# Optimizing a Trainium2 kernel written in Bass

```python
import jax, jax.numpy as jnp
from jax import lax
import numpy as np

D_MODEL = 2048
BATCH = 1
SEQ = 256
DEPTH = 2

N_MIXERS = 2
POOL_WINDOWS = (2, 4, 8, 16)
N_POOL_GROUPS = 4
POOL_GROUP_DIM = D_MODEL // N_POOL_GROUPS
HEAD_DIM = 128
N_HEADS = D_MODEL // HEAD_DIM
Q_BLOCK = 128
D_FF = 5504
CONV_WIDTH = 3
LN_EPS = 1e-5
DEEPNORM_ALPHA = (2.0 * DEPTH) ** 0.25
DEEPNORM_BETA = (8.0 * DEPTH) ** -0.25
N_POOL_LAYERS = (DEPTH + 1) // 2
N_ATTN_LAYERS = DEPTH // 2

kernel_name = "hybrid_pool_stickbreak_convffn_deepnorm"

def layer_norm(x, g, b):
    xf = x.astype(jnp.float32)
    mu = jnp.mean(xf, axis=-1, keepdims=True)
    var = jnp.mean(jnp.square(xf - mu), axis=-1, keepdims=True)
    y = (xf - mu) * lax.rsqrt(var + LN_EPS)
    return (y * g.astype(jnp.float32) + b.astype(jnp.float32)).astype(x.dtype)

def pool_mixer(x, w_groups, scale):
    B, S, D = x.shape
    xf = x.astype(jnp.float32)
    cs = jnp.cumsum(xf, axis=1).reshape(B, S, N_POOL_GROUPS, POOL_GROUP_DIM)
    xg = xf.reshape(B, S, N_POOL_GROUPS, POOL_GROUP_DIM)
    t1 = jnp.arange(1, S + 1)
    outs = []
    for g, w in enumerate(POOL_WINDOWS):
        c = cs[:, :, g]
        shifted = jnp.pad(c, ((0, 0), (w, 0), (0, 0)))[:, :S]
        cnt = jnp.minimum(t1, w).astype(jnp.float32)[None, :, None]
        outs.append((c - shifted) / cnt - xg[:, :, g])
    pooled = jnp.stack(outs, axis=2).astype(x.dtype)
    y = jnp.einsum('bsgc,gcd->bsgd', pooled, w_groups).reshape(B, S, D)
    return y * scale

def stick_breaking_attention(x, w_qkv, w_o):
    B, S, D = x.shape
    qkv = x @ w_qkv
    q, k, v = jnp.split(qkv, 3, axis=-1)
    nb = S // Q_BLOCK
    q_blocks = q.reshape(B, nb, Q_BLOCK, N_HEADS, HEAD_DIM).transpose(1, 0, 3, 2, 4)
    k = k.reshape(B, S, N_HEADS, HEAD_DIM).transpose(0, 2, 1, 3)
    v = v.reshape(B, S, N_HEADS, HEAD_DIM).transpose(0, 2, 1, 3)
    k_pos = jnp.arange(S)
    scale = HEAD_DIM ** -0.5

    def block(args):
        qb, bi = args
        z = jnp.einsum('bhqd,bhkd->bhqk', qb, k).astype(jnp.float32) * scale
        q_pos = bi * Q_BLOCK + jnp.arange(Q_BLOCK)
        mask = k_pos[None, :] < q_pos[:, None]
        log_not = jnp.where(mask, jax.nn.log_sigmoid(-z), 0.0)
        rest = lax.cumsum(log_not, axis=3, reverse=True)
        log_a = jnp.where(mask, z + rest, -jnp.inf)
        a = jnp.exp(log_a)
        return jnp.einsum('bhqk,bhkd->bhqd', a.astype(v.dtype), v)

    o = lax.map(block, (q_blocks, jnp.arange(nb)))
    o = o.transpose(1, 0, 3, 2, 4).reshape(B, S, D)
    return o @ w_o

def conv_ffn(x, w_up, conv_w, conv_b, w_down):
    S = x.shape[1]
    h = x @ w_up
    hp = jnp.pad(h, ((0, 0), (CONV_WIDTH - 1, 0), (0, 0)))
    hc = conv_b + conv_w[0] * hp[:, 0:S]
    for kk in range(1, CONV_WIDTH):
        hc = hc + conv_w[kk] * hp[:, kk:kk + S]
    gate, val = jnp.split(hc, 2, axis=-1)
    return (jax.nn.silu(gate) * val) @ w_down

def setup_inputs(seed: int = 0) -> dict:
    key = jax.random.key(seed)
    ks = jax.random.split(key, 14)
    f32 = jnp.float32
    nrm = lambda k, shp: jax.random.normal(k, shp, dtype=f32)
    x = nrm(ks[0], (BATCH, SEQ, D_MODEL))
    pool_w = nrm(ks[1], (N_POOL_LAYERS, N_POOL_GROUPS, POOL_GROUP_DIM, POOL_GROUP_DIM)) * (POOL_GROUP_DIM ** -0.5) * DEEPNORM_BETA
    pool_scale = 1.0 + 0.02 * nrm(ks[2], (N_POOL_LAYERS, D_MODEL))
    attn_w_qkv = nrm(ks[3], (N_ATTN_LAYERS, D_MODEL, 3 * D_MODEL)) * (D_MODEL ** -0.5)
    attn_w_o = nrm(ks[4], (N_ATTN_LAYERS, D_MODEL, D_MODEL)) * (D_MODEL ** -0.5) * DEEPNORM_BETA
    ffn_w_up = nrm(ks[5], (DEPTH, D_MODEL, 2 * D_FF)) * (D_MODEL ** -0.5)
    ffn_conv_w = nrm(ks[6], (DEPTH, CONV_WIDTH, 2 * D_FF)) * (CONV_WIDTH ** -0.5)
    ffn_conv_b = 0.02 * nrm(ks[7], (DEPTH, 2 * D_FF))
    ffn_w_down = nrm(ks[8], (DEPTH, D_FF, D_MODEL)) * (D_FF ** -0.5) * DEEPNORM_BETA
    ln_mix_g = 1.0 + 0.02 * nrm(ks[9], (DEPTH, D_MODEL))
    ln_mix_b = 0.02 * nrm(ks[10], (DEPTH, D_MODEL))
    ln_ffn_g = 1.0 + 0.02 * nrm(ks[11], (DEPTH, D_MODEL))
    ln_ffn_b = 0.02 * nrm(ks[12], (DEPTH, D_MODEL))
    return {"x": x, "pool_w": pool_w, "pool_scale": pool_scale,
            "attn_w_qkv": attn_w_qkv, "attn_w_o": attn_w_o,
            "ffn_w_up": ffn_w_up, "ffn_conv_w": ffn_conv_w, "ffn_conv_b": ffn_conv_b,
            "ffn_w_down": ffn_w_down, "ln_mix_g": ln_mix_g, "ln_mix_b": ln_mix_b,
            "ln_ffn_g": ln_ffn_g, "ln_ffn_b": ln_ffn_b}

def reference(x, pool_w, pool_scale, attn_w_qkv, attn_w_o, ffn_w_up, ffn_conv_w,
              ffn_conv_b, ffn_w_down, ln_mix_g, ln_mix_b, ln_ffn_g, ln_ffn_b):
    for i in range(DEPTH):
        j = i // N_MIXERS
        if i % N_MIXERS == 0:
            y = pool_mixer(x, pool_w[j], pool_scale[j])
        else:
            y = stick_breaking_attention(x, attn_w_qkv[j], attn_w_o[j])
        x = layer_norm(DEEPNORM_ALPHA * x + y, ln_mix_g[i], ln_mix_b[i])
        f = conv_ffn(x, ffn_w_up[i], ffn_conv_w[i], ffn_conv_b[i], ffn_w_down[i])
        x = layer_norm(DEEPNORM_ALPHA * x + f, ln_ffn_g[i], ln_ffn_b[i])
    return x


_drawn_inputs = setup_inputs


def setup_inputs(seed=0):
    import zlib

    import numpy as np

    out = dict(_drawn_inputs(seed))
    spreads = {}
    factors = {'pool_scale': 22.549, 'ffn_conv_b': 6.666}
    for name, (base, spread) in spreads.items():
        noise = np.random.default_rng([zlib.crc32(name.encode()), seed]).standard_normal(out[name].shape)
        drawn = base * np.exp(spread * noise) if base else spread * noise
        out[name] = __import__('jax').numpy.asarray(drawn.astype(out[name].dtype))
    for name, factor in factors.items():
        out[name] = (out[name] * factor).astype(out[name].dtype)
    return out
```

```python
import concourse.bass as bass
from concourse import mybir
from contextlib import ExitStack


def decoder_trunk(nc, x, pool_w, pool_scale, attn_w_qkv, attn_w_o, ffn_w_up, ffn_conv_w, ffn_conv_b,
                  ffn_w_down, ln_mix_g, ln_mix_b, ln_ffn_g, ln_ffn_b, out):
    f32 = mybir.dt.float32
    f32r = mybir.dt.float32r
    ALU = mybir.AluOpType
    ACT = mybir.ActivationFunctionType
    AX = mybir.AxisListType

    P = 128
    T = x.shape[1]
    D = x.shape[2]
    DEPTH = ffn_w_up.shape[0]
    FF = ffn_w_down.shape[1]
    TT = T // P
    XT = D // P
    FT = FF // P
    CT = 4
    KT = 4
    WC = CT * P
    NG = XT // CT
    TAPS = ffn_conv_w.shape[1]
    ALPHA = float((2.0 * DEPTH) ** 0.25)
    EPS = 1e-5
    ZSCALE = float(P) ** -0.5
    WINDOWS = (2, 4, 8, 16)
    PAD = WINDOWS[-1]
    FIRST = CT * P
    assert (T, TT, XT, NG, TAPS, DEPTH) == (2 * P, 2, 16, 4, 3, 2) and FF == FT * P

    UJ = -(-FT // CT)
    LAST_TILES = FT - (UJ - 1) * CT
    D_ROWS = [KT] * (XT // KT)
    DOWN_ROWS = [3, 3, 3, 2] + [4] * 8
    assert sum(DOWN_ROWS) == FT and len(DOWN_ROWS) % 4 == 0
    DC, FC = len(D_ROWS), len(DOWN_ROWS)

    names = ["pool", "up0", "down0", "qkv", "attn_out", "up1", "down1", "end"]
    chunks = [NG, 2 * UJ * DC, NG * FC, 3 * NG * DC, NG * DC, 2 * UJ * DC, NG * FC]
    groups = [NG, 2 * UJ, NG, 3 * NG, NG, 2 * UJ, NG]
    C0 = {n: sum(chunks[:i]) for i, n in enumerate(names)}
    G0 = {n: sum(groups[:i]) for i, n in enumerate(names)}
    assert all(c % 4 == 0 for c in C0.values())

    ctx = ExitStack()
    with ctx:
        top = [-(-nc.sbuf_base // 64) * 64]

        def at(name, shape, dtype, offset):
            return nc.alloc_sbuf_tensor_at(name, shape, dtype, offset=offset)

        def place(name, shape, dtype):
            size = 4
            for n in shape[1:]:
                size *= n
            t = at(name, shape, dtype, top[0])
            top[0] += -(-size // 64) * 64
            return t

        raw = [place(f"raw{i}", [P, KT, WC], f32) for i in range(4)]
        high = [place(f"weights_high{i}", [P, KT, WC], f32r) for i in range(2)]
        low = [place(f"weights_low{i}", [P, KT, WC], f32r) for i in range(2)]
        xs = place("xs", [P, XT, 2 * T], f32r)
        r_at = top[0]
        r = place("r", [P, XT, T], f32)
        gs_at = top[0]
        gs = place("gs", [P, FT, 2 * T], f32r)
        cross = place("cross", [P, 2, T], f32)
        total = place("total", [P, 2, T], f32)
        centre = place("centre", [P, T], f32)
        sum_c = place("sum_c", [P, T], f32)
        sum_q = place("sum_q", [P, T], f32)
        squares = place("squares", [P, 4, T], f32)
        shift = place("shift", [P, T], f32)
        variance = place("variance", [P, T], f32)
        deviation = place("deviation", [P, T], f32)
        rstd = place("rstd", [P, T], f32)
        ident = place("ident", [P, P], f32)
        mean_w = place("mean_w", [P, P], f32)
        tri_w = place("tri_w", [P, P], f32)
        convp = place("convp", [P, 4 * DEPTH, 2 * FT], f32)
        lnp = place("lnp", [P, 4, DEPTH, XT], f32)
        pscale = place("pscale", [P, XT], f32)
        count = place("count", [P, PAD], f32)
        eps = place("eps", [P, 1], f32)
        assert top[0] <= nc.sbuf_usable_end

        hidden = at("hidden", [P, 2, T + 2], f32, r_at)
        convs = at("convs", [P, 2, T], f32, r_at + 2112)
        gate = at("gate", [P, CT, T], f32, r_at + 4160)
        value = at("value", [P, CT, T], f32, r_at + 8256)
        free = gs_at + XT * 2 * T * 4
        x_in = at("x_in", [P, TT, D], f32, free)
        x_pad = at("x_pad", [P, XT, PAD + T], f32, free + 16384)
        window_a = at("window_a", [P, CT, PAD + T], f32, free + 33792)
        window_b = at("window_b", [P, CT, PAD + T], f32, free + 38144)
        pooled = at("pooled", [P, CT, T], f32, free + 42496)
        conv_in = at("conv_in", [2 * FT, 4 * DEPTH, P], f32, free + 46592)
        ln_in = at("ln_in", [P, P], f32, free + 50688)
        pscale_in = at("pscale_in", [XT, P], f32, free + 51200)
        v_t = at("v_t", [P, CT, T], f32, free)
        q_t = at("q_t", [P, CT, T], f32, free + 4096)
        k_t = at("k_t", [P, CT, T], f32, free + 8192)
        v_n = at("v_n", [P, CT, T], f32, free + 12288)
        z = at("z", [P, CT, 3 * P], f32, free + 16384)
        soft = at("soft", [P, CT, 3 * P], f32, free + 22528)
        o_sb = at("o_sb", [P, TT, D], f32, gs_at)

        bank = [ctx.enter_context(nc.psum_tensor(f"bank{i}", [P, WC], f32)) for i in range(8)]

        def sem(name):
            return ctx.enter_context(nc.semaphore(name))

        weights_loaded = [sem(f"weights_loaded{i}") for i in range(4)]
        weights_high = sem("weights_high_ready")
        weights_split = sem("weights_split")
        tiles_multiplied = sem("tiles_multiplied")
        cross_copied = sem("cross_copied")
        evacuated = sem("evacuated")
        x_loaded, params_loaded = sem("x_loaded"), sem("params_loaded")
        consts_ready = sem("consts_ready")
        pads_zeroed = sem("pads_zeroed")
        x_transposed, x_padded = sem("x_transposed"), sem("x_padded")
        params_transposed, params_copied = sem("params_transposed"), sem("params_copied")
        pool_ready, pool_high, pool_split = sem("pool_ready"), sem("pool_high"), sem("pool_split")
        part_summed = sem("part_summed")
        centre_multiplied, centre_copied = sem("centre_multiplied"), sem("centre_copied")
        half_prepared, prepared = sem("half_prepared"), sem("prepared")
        centred = sem("centred")
        squared = sem("squared")
        sums_c, sums_q = sem("sums_c"), sem("sums_q")
        stats_multiplied = sem("stats_multiplied")
        variance_ready, deviation_ready = sem("variance_ready"), sem("deviation_ready")
        normalized = sem("normalized")
        affine = sem("affine")
        x_high, x_split = sem("x_high"), sem("x_split")
        first_tap, middle_tap, convolved = sem("first_tap"), sem("middle_tap"), sem("convolved")
        silu_done, products, inner_high, inner_split = (
            sem("silu_done"), sem("products"), sem("inner_high"), sem("inner_split"))
        heads_multiplied = sem("heads_multiplied")
        v_copied, z_copied = sem("v_copied"), sem("z_copied")
        z_abs, z_exp, z_log, softplus = sem("z_abs"), sem("z_exp"), sem("z_log"), sem("softplus")
        masked = sem("masked")
        log_weights, weights_exp = sem("log_weights"), sem("weights_exp")
        heads_high, heads_split = sem("heads_high"), sem("heads_split")
        out_transposed, out_copied, out_stored = sem("out_transposed"), sem("out_copied"), sem("out_stored")
        vector_steps = sem("vector_steps")

        block = ctx.enter_context(nc.Block())

        def halves(tiles):
            return (slice(0, 2 * P), slice(2 * P, tiles * P))

        def group_tiles(j):
            return LAST_TILES if isinstance(j, int) and j == UJ - 1 else CT

        def steps_of(ct, tiles):
            return CT - ct if ct == tiles - 1 else 1

        @block.sync
        def _(sp):
            sp.dma_start(x_in[:, :, :], x[0].rearrange("(t p) d -> p t d", p=P)).then_inc(x_loaded, 16)

            def load(c0, k, matrix, row_tile, rows, col, tiles=CT):
                c = c0 + k
                if not (isinstance(c, int) and c < 4):
                    sp.wait_ge(weights_split, 2 * (c - 4) + 2)
                source = matrix[row_tile * P:(row_tile + rows) * P, bass.ds(col, tiles * P)]
                sp.dma_start(raw[k % 4][:, 0:rows, 0:tiles * P],
                             source.rearrange("(t p) n -> p t n", p=P)).then_inc(weights_loaded[k % 4], 16)

            def load_up(layer, c0, j):
                for k in range(2 * DC):
                    half = k // DC
                    load(c0 + 2 * DC * j, k, ffn_w_up[layer], (k % DC) * KT, KT,
                         half * FF + j * WC, group_tiles(j))

            def load_down(layer, c0):
                with sp.Fori(0, NG) as dg:
                    for k in range(FC):
                        load(c0 + FC * dg, k, ffn_w_down[layer], sum(DOWN_ROWS[:k]), DOWN_ROWS[k], dg * WC)

            for g in range(NG):
                load(0, g, pool_w[0, g], 0, KT, 0)
            for layer in range(DEPTH):
                up = C0[f"up{layer}"]
                with sp.Fori(0, UJ - 1) as j:
                    load_up(layer, up, j)
                load_up(layer, up, UJ - 1)
                load_down(layer, C0[f"down{layer}"])
                if layer == 0:
                    qkv = attn_w_qkv[0].rearrange("k (s n) -> s k n", s=3)
                    with sp.Fori(1, NG + 1) as g:
                        for n, part in enumerate((2, 0, 1)):
                            for k in range(DC):
                                load(C0["qkv"] + 3 * DC * g - 3 * DC, n * DC + k, qkv[part], k * KT, KT,
                                     g * WC - WC)
                    with sp.Fori(0, NG) as dg:
                        for k in range(DC):
                            load(C0["attn_out"] + DC * dg, k, attn_w_o[0], k * KT, KT, dg * WC)
            for n in range(2 * NG):
                dq, tt = n // 2, n % 2
                sp.wait_ge(out_copied, n + 1)
                sp.dma_start(out[0, tt * P:(tt + 1) * P, dq * WC:(dq + 1) * WC],
                             o_sb[:, tt, dq * WC:(dq + 1) * WC]).then_inc(out_stored, 16)
            sp.wait_ge(out_stored, 16 * 2 * NG)

        @block.gpsimd
        def _(pool):
            nc.gpsimd.memset(ident[:, :], 0.0).then_inc(consts_ready, 1)
            nc.gpsimd.memset(mean_w[:, :], 1.0 / FIRST).then_inc(consts_ready, 1)
            nc.gpsimd.memset(tri_w[:, :], 1.0 / FIRST).then_inc(consts_ready, 1)
            nc.gpsimd.memset(eps[:, :], EPS).then_inc(consts_ready, 1)
            for t in range(PAD):
                nc.gpsimd.memset(count[:, t:t + 1], 1.0 / (t + 1)).then_inc(consts_ready, 1)
            pool.wait_ge(consts_ready, 4 + PAD)
            nc.gpsimd.affine_select(out=ident[:, :], in_=ident[:, :], compare_op=ALU.not_equal, fill=1.0,
                                    base=0, pattern=[[-1, P]], channel_multiplier=1).then_inc(consts_ready, 1)
            nc.gpsimd.affine_select(out=tri_w[:, :], in_=tri_w[:, :], compare_op=ALU.is_ge, fill=0.0,
                                    base=0, pattern=[[-1, P]], channel_multiplier=1).then_inc(consts_ready, 1)

            def mask(tile, block_at):
                part = tile[:, :, block_at * P:(block_at + 1) * P]
                nc.gpsimd.affine_select(out=part, in_=part, compare_op=ALU.is_gt, fill=0.0, base=0,
                                        pattern=[[0, CT], [1, P]], channel_multiplier=-1).then_inc(masked, 1)

            for g in range(NG):
                pool.wait_ge(softplus, g + 1)
                mask(soft, 0)
                mask(soft, 2)
                pool.wait_ge(weights_exp, g + 1)
                mask(z, 0)
                mask(z, 2)

        @block.scalar
        def _(act):
            for layer in range(DEPTH):
                for n, source in enumerate([ffn_conv_w[layer, i] for i in range(TAPS)] + [ffn_conv_b[layer]]):
                    act.dma_start(conv_in[:, 4 * layer + n, :],
                                  source.rearrange("(t p) -> t p", p=P)).then_inc(params_loaded, 16)
            for n, source in enumerate((ln_mix_g, ln_mix_b, ln_ffn_g, ln_ffn_b)):
                act.dma_start(ln_in[n * DEPTH * XT:(n + 1) * DEPTH * XT, :],
                              source.rearrange("l (t p) -> (l t) p", p=P)).then_inc(params_loaded, 16)
            act.dma_start(pscale_in[:, :], pool_scale[0].rearrange("(t p) -> t p", p=P)).then_inc(params_loaded, 16)

            def take_high(c0, k, rows=KT, tiles=CT):
                c = c0 + k
                act.wait_ge(weights_loaded[k % 4], 16 * (c0 // 4 if isinstance(c0, int) else 0) + 16 * (k // 4 + 1)
                            if isinstance(c0, int) else 4 * (c0 - 0) + 16 * (k // 4 + 1))
                for h, cols in enumerate(halves(tiles)):
                    if not (isinstance(c, int) and c < 2):
                        act.wait_ge(tiles_multiplied, 4 * (c - 2) + 2 * h + 2)
                    nc.scalar.activation(high[k % 2][:, 0:rows, cols], raw[k % 4][:, 0:rows, cols],
                                         ACT.Copy).then_inc(weights_high, 1)

            def copy_cross(G, c_end, ct, tiles=CT, banks=0, scale=None):
                act.wait_ge(tiles_multiplied, 4 * c_end + ct + 1)
                if not (isinstance(G, int) and G == 0 and ct < 2):
                    act.wait_ge(evacuated, 4 * G + ct - 1)
                source = bank[banks + ct][:, T:2 * T]
                if scale is None:
                    op = nc.scalar.activation(cross[:, ct % 2, :], source, ACT.Copy)
                else:
                    op = nc.scalar.activation(cross[:, ct % 2, :], source, ACT.Identity, scale=scale)
                op.then_inc(cross_copied, steps_of(ct, tiles))

            def square(L, i):
                act.wait_ge(centred, XT * L + i + 1)
                if not (isinstance(i, int) and i < 4):
                    act.wait_ge(sums_q, 12 * L + i - 3)
                return i

            def squares_of(L, dg, ct):
                i = CT * dg + ct
                act.wait_ge(centred, XT * L + i + 1)
                if not (isinstance(dg, int) and dg == 0):
                    act.wait_ge(sums_q, 12 * L + i - 3)
                nc.scalar.activation(squares[:, ct, :], r[:, bass.ds(i, 1), :].rearrange("p o t -> p (o t)"),
                                     ACT.Square).then_inc(squared, 1)

            def empty_residual(L, G, dg, c_end, scaled=False):
                for ct in range(CT):
                    i = CT * dg + ct
                    copy_cross(G, c_end, ct, scale=pscale[:, i:i + 1] if scaled else None)
                    if ct and not (isinstance(dg, int) and dg == 0):
                        squares_of(L, dg, ct - 1)
                if not (isinstance(dg, int) and dg == 0):
                    squares_of(L, dg, CT - 1)

            def copy_centre(L):
                act.wait_ge(centre_multiplied, L + 1)
                nc.scalar.activation(centre[:, :], bank[4][:, 0:T], ACT.Copy).then_inc(centre_copied, 1)
                for ct in range(CT):
                    squares_of(L, 0, ct)

            def finish_norm(L, last=False):
                which, layer = (0 if L % 2 == 0 else 2), L // 2
                act.wait_ge(variance_ready, L + 1)
                nc.scalar.activation(deviation[:, :], variance[:, :], ACT.Sqrt, bias=eps[:, :]).then_inc(deviation_ready, 1)
                for b in range(XT // 2):
                    act.wait_ge(normalized, 8 * L + b + 1)
                    for i in (2 * b, 2 * b + 1):
                        nc.scalar.activation(r[:, i, :], r[:, i, :], ACT.Identity,
                                             scale=lnp[:, which, layer, i:i + 1],
                                             bias=lnp[:, which + 1, layer, i:i + 1]).then_inc(affine, 1)
                    if not last:
                        act.wait_ge(affine, XT * L + 2 * b + 2)
                        nc.scalar.activation(xs[:, 2 * b:2 * b + 2, 0:T], r[:, 2 * b:2 * b + 2, :],
                                             ACT.Copy).then_inc(x_high, 1)

            for b in range(8):
                act.wait_ge(x_transposed, b + 1)
                nc.scalar.activation(x_pad[:, 2 * b:2 * b + 2, PAD:PAD + T],
                                     bank[b][:, :].rearrange("p (i t) -> p i t", i=2), ACT.Copy).then_inc(x_padded, 1)
            act.wait_ge(params_transposed, 4)
            for layer in range(DEPTH):
                nc.scalar.activation(convp[:, 4 * layer:4 * layer + 4, :],
                                     bank[layer][:, 0:4 * 2 * FT].rearrange("p (n t) -> p n t", n=4),
                                     ACT.Copy).then_inc(params_copied, 1)
            nc.scalar.activation(lnp[:, :, :, :], bank[2][:, 0:P].rearrange("p (n l t) -> p n l t", n=4, l=DEPTH),
                                 ACT.Copy).then_inc(params_copied, 1)
            nc.scalar.activation(pscale[:, :], bank[3][:, 0:XT], ACT.Copy).then_inc(params_copied, 1)
            act.wait_ge(params_copied, 4)
            take_high(0, 0)
            take_high(0, 1)
            for g in range(NG):
                act.wait_ge(x_padded, 8)
                nc.scalar.activation(xs[:, CT * g:CT * g + CT, 0:T], x_pad[:, CT * g:CT * g + CT, PAD:PAD + T],
                                     ACT.Copy).then_inc(x_high, 1)
                act.wait_ge(pool_ready, g + 1)
                nc.scalar.activation(gs[:, CT * g:CT * g + CT, 0:T], pooled[:, :, :], ACT.Copy).then_inc(pool_high, 1)
            empty_residual(0, 0, 0, 0, scaled=True)
            take_high(0, 2)
            copy_centre(0)
            empty_residual(0, 1, 1, 1, scaled=True)
            take_high(0, 3)
            empty_residual(0, 2, 2, 2, scaled=True)
            take_high(C0["up0"], 0)
            empty_residual(0, 3, 3, 3, scaled=True)
            take_high(C0["up0"], 1)
            finish_norm(0)

            def up_cross(layer, j, half):
                tiles = group_tiles(j)
                G = G0[f"up{layer}"] + 2 * j + half
                c_end = C0[f"up{layer}"] + 2 * DC * j + DC * (half + 1) - 1
                n = (2 * UJ + 1) * CT * layer + CT + CT * (2 * j + half)

                def tap(ct):
                    col = half * FT + j * CT + ct
                    act.wait_ge(evacuated, 4 * G + ct + 1)
                    act.wait_ge(convolved, n + ct - 1)
                    nc.scalar.activation(convs[:, ct % 2, :], hidden[:, ct % 2, 2:2 + T], ACT.Identity,
                                         scale=convp[:, 4 * layer + 2, bass.ds(col, 1)],
                                         bias=convp[:, 4 * layer + 3, bass.ds(col, 1)]
                                         ).then_inc(first_tap, steps_of(ct, tiles))

                for ct in range(tiles):
                    copy_cross(G, c_end, ct, tiles, banks=4 * half)
                    if ct:
                        tap(ct - 1)
                tap(tiles - 1)

            def apply_silu(layer, j):
                tiles = group_tiles(j)
                act.wait_ge(convolved, (2 * UJ + 1) * CT * layer + CT + CT * (2 * j + 1))
                nc.scalar.activation(gate[:, 0:tiles, :], gate[:, 0:tiles, :], ACT.Silu).then_inc(silu_done, 1)

            def take_inner_high(layer, j):
                tiles = group_tiles(j)
                act.wait_ge(products, UJ * layer + j + 1)
                nc.scalar.activation(gs[:, bass.ds(j * CT, tiles), 0:T], value[:, 0:tiles, :],
                                     ACT.Copy).then_inc(inner_high, 1)

            def up_group(layer, j, first=False):
                c0, tiles = C0[f"up{layer}"] + 2 * DC * j, group_tiles(j)
                for k in range(2 * DC):
                    if not (first and k < 2):
                        take_high_at(c0, k, tiles=tiles)
                    if k == 0 and not first:
                        up_cross(layer, j - 1, 1)
                    if k == 2 and not first:
                        take_inner_high(layer, j - 1)
                    if k == 4:
                        up_cross(layer, j, 0)
                    if k == 5:
                        apply_silu(layer, j)

            def take_high_at(c0, k, rows=KT, tiles=CT):
                c = c0 + k
                act.wait_ge(weights_loaded[k % 4], 4 * c0 + 16 * (k // 4 + 1))
                for h, cols in enumerate(halves(tiles)):
                    act.wait_ge(tiles_multiplied, 4 * (c - 2) + 2 * h + 2)
                    nc.scalar.activation(high[k % 2][:, 0:rows, cols], raw[k % 4][:, 0:rows, cols],
                                         ACT.Copy).then_inc(weights_high, 1)

            for layer in range(DEPTH):
                up_group(layer, 0, first=True)
                with act.Fori(1, UJ - 1) as j:
                    up_group(layer, j)
                up_group(layer, UJ - 1)
                c0, g0, L = C0[f"down{layer}"], G0[f"down{layer}"], 2 * layer + 1

                def down_group(dg):
                    for k in range(FC):
                        take_high_at(c0 + FC * dg, k, DOWN_ROWS[k])
                        if isinstance(dg, int) and dg == 0:
                            if k == 0:
                                up_cross(layer, UJ - 1, 1)
                            if k == 2:
                                take_inner_high(layer, UJ - 1)
                        elif k == 0:
                            empty_residual(L, g0 + dg - 1, dg - 1, c0 + FC * dg - 1)
                        if isinstance(dg, int) and dg == 1 and k == 2:
                            copy_centre(L)

                down_group(0)
                down_group(1)
                with act.Fori(2, NG) as dg:
                    down_group(dg)
                if layer == 1:
                    empty_residual(L, g0 + NG - 1, NG - 1, c0 + FC * NG - 1)
                    finish_norm(L, last=True)
                    break
                take_high_at(C0["qkv"], 0)
                empty_residual(L, g0 + NG - 1, NG - 1, c0 + FC * NG - 1)
                take_high_at(C0["qkv"], 1)
                finish_norm(L)

                def cross_of(g, part):
                    for ct in range(CT):
                        copy_cross(G0["qkv"] + 3 * g + part, C0["qkv"] + 3 * DC * g + DC * (part + 1) - 1, ct)

                def score_functions(g):
                    for h in range(CT):
                        act.wait_ge(heads_multiplied, 16 * g + 4 + h + 1)
                        nc.scalar.activation(z[:, h, :], bank[4 + h][:, 0:3 * P], ACT.Copy,
                                             scale=ZSCALE).then_inc(z_copied, 1)
                    act.wait_ge(z_abs, g + 1)
                    nc.scalar.activation(soft[:, :, :], soft[:, :, :], ACT.Exp, scale=-1.0).then_inc(z_exp, 1)
                    act.wait_ge(z_exp, g + 1)
                    nc.scalar.activation(soft[:, :, :], soft[:, :, :], ACT.Ln, bias=1.0).then_inc(z_log, 1)

                def weight_functions(g):
                    act.wait_ge(log_weights, 4 * g + 4)
                    nc.scalar.activation(z[:, :, :], z[:, :, :], ACT.Exp).then_inc(weights_exp, 1)

                def take_heads_high(g):
                    for h in range(CT):
                        act.wait_ge(heads_multiplied, 16 * g + 12 + h + 1)
                        nc.scalar.activation(gs[:, bass.ds(CT * g + h, 1), 0:T].rearrange("p o t -> p (o t)"),
                                             bank[4 + h][:, 0:T], ACT.Copy).then_inc(heads_high, 1)

                def copy_values(g):
                    for h in range(CT):
                        act.wait_ge(heads_multiplied, 16 * g + h + 1)
                        nc.scalar.activation(v_n[:, h, :], bank[4 + h][:, 0:T], ACT.Copy).then_inc(v_copied, 1)

                def qkv_group(g, first=False):
                    c = C0["qkv"] + 3 * DC * g
                    for k in range(3 * DC):
                        if not (first and k < 2):
                            take_high_at(c, k)
                        if k == 0 and not first:
                            cross_of(g - 1, 2)
                        if k == 2 and not first:
                            score_functions(g - 1)
                        if k == 4:
                            if not first:
                                weight_functions(g - 1)
                            cross_of(g, 0)
                        if k == 6 and not first:
                            take_heads_high(g - 1)
                        if k == 8:
                            copy_values(g)
                            cross_of(g, 1)

                qkv_group(0, first=True)
                with act.Fori(1, NG) as g:
                    qkv_group(g)

                def attn_out_group(dg):
                    c = C0["attn_out"] + DC * dg
                    for k in range(DC):
                        take_high_at(c, k)
                        if isinstance(dg, int) and dg == 0:
                            if k == 0:
                                cross_of(NG - 1, 2)
                            if k == 2:
                                score_functions(NG - 1)
                                weight_functions(NG - 1)
                                take_heads_high(NG - 1)
                        elif k == 0:
                            empty_residual(2, G0["attn_out"] + dg - 1, dg - 1, c - 1)
                        if isinstance(dg, int) and dg == 1 and k == 2:
                            copy_centre(2)

                attn_out_group(0)
                attn_out_group(1)
                with act.Fori(2, NG) as dg:
                    attn_out_group(dg)
                take_high_at(C0["up1"], 0)
                empty_residual(2, G0["attn_out"] + NG - 1, NG - 1, C0["up1"] - 1)
                take_high_at(C0["up1"], 1)
                finish_norm(2)

        @block.vector
        def _(dve):
            steps = [0]

            def step(instruction):
                steps[0] += 1
                instruction.then_inc(vector_steps, 1)
                dve.wait_ge(vector_steps, steps[0])

            def take_low(c, k, rows=KT, tiles=CT):
                for h, cols in enumerate(halves(tiles)):
                    dve.wait_ge(weights_high, 2 * c + h + 1)
                    nc.vector.tensor_tensor(low[k % 2][:, 0:rows, cols], raw[k % 4][:, 0:rows, cols],
                                            high[k % 2][:, 0:rows, cols].bitcast(f32),
                                            ALU.subtract).then_inc(weights_split, 1)

            def add_terms(G, ct, dst, tiles=CT, banks=0, scale=1.0):
                dve.wait_ge(cross_copied, 4 * G + ct + 1)
                if isinstance(scale, float):
                    op = nc.vector.tensor_tensor(dst, bank[banks + ct][:, 0:T], cross[:, ct % 2, :], ALU.add)
                else:
                    op = nc.vector.scalar_tensor_tensor(out=dst, in0=bank[banks + ct][:, 0:T], scalar=scale,
                                                        in1=cross[:, ct % 2, :], op0=ALU.mult, op1=ALU.add)
                op.then_inc(evacuated, steps_of(ct, tiles))

            def per_tile(t, n):
                return t.unsqueeze(1).broadcast_to([P, n, T])

            def prepare(L, dg):
                part = bass.ds(CT * dg, CT)
                x_low, x_hi = xs[:, part, T:2 * T].bitcast(f32), xs[:, part, 0:T].bitcast(f32)
                if isinstance(dg, int) and dg == 0:
                    op = nc.vector.tensor_scalar(r[:, part, :], x_low, ALPHA, None, ALU.mult)
                else:
                    dve.wait_ge(centre_copied, L + 1)
                    op = nc.vector.scalar_tensor_tensor(out=r[:, part, :], in0=x_low, scalar=ALPHA,
                                                        in1=per_tile(centre[:, :], CT),
                                                        op0=ALU.mult, op1=ALU.subtract)
                op.then_inc(half_prepared, 1)
                dve.wait_ge(half_prepared, NG * L + dg + 1)
                nc.vector.scalar_tensor_tensor(out=r[:, part, :], in0=x_hi, scalar=ALPHA, in1=r[:, part, :],
                                               op0=ALU.mult, op1=ALU.add).then_inc(prepared, 1)

            def row(i):
                return r[:, bass.ds(i, 1), :].rearrange("p o t -> p (o t)")

            def empty_first(L, G, scaled=False):
                for ct in range(CT + 1):
                    if ct < CT:
                        if ct > 1:
                            dve.wait_ge(vector_steps, steps[0])
                        add_terms(G, ct, total[:, ct % 2, :], scale=pscale[:, ct:ct + 1] if scaled else 1.0)
                    if ct:
                        n = ct - 1
                        dve.wait_ge(evacuated, 4 * G + n + 1)
                        dve.wait_ge(prepared, NG * L + 1)
                        nc.vector.tensor_tensor(r[:, n, :], total[:, n % 2, :], r[:, n, :],
                                                ALU.add).then_inc(vector_steps, 1)
                        steps[0] += 1
                dve.wait_ge(vector_steps, steps[0])
                nc.vector.tensor_reduce(out=sum_c[:, :], in_=r[:, 0:CT, :].rearrange("p i t -> p t i"),
                                        axis=AX.X, op=ALU.add).then_inc(part_summed, 1)

            def centre_first(L):
                dve.wait_ge(centre_copied, L + 1)
                nc.vector.tensor_tensor(r[:, 0:CT, :], r[:, 0:CT, :], per_tile(centre[:, :], CT),
                                        ALU.subtract).then_inc(centred, CT)
                dve.wait_ge(centred, XT * L + CT)
                nc.vector.tensor_reduce(out=sum_c[:, :], in_=r[:, 0:CT, :].rearrange("p i t -> p t i"),
                                        axis=AX.X, op=ALU.add).then_inc(sums_c, CT)
                dve.wait_ge(squared, XT * L + 2)
                nc.vector.tensor_tensor(sum_q[:, :], squares[:, 0, :], squares[:, 1, :], ALU.add).then_inc(sums_q, 2)
                for i in (2, 3):
                    add_square(L, i, i)

            def add_centred(L, i):
                dve.wait_ge(sums_c, 12 * L + i)
                dve.wait_ge(centred, XT * L + i + 1)
                nc.vector.tensor_tensor(sum_c[:, :], sum_c[:, :], row(i), ALU.add).then_inc(sums_c, 1)

            def add_square(L, i, ct):
                dve.wait_ge(squared, XT * L + i + 1)
                dve.wait_ge(sums_q, 12 * L + i)
                nc.vector.tensor_tensor(sum_q[:, :], sum_q[:, :], squares[:, ct, :], ALU.add).then_inc(sums_q, 1)

            def empty_residual(L, G, dg, scaled=False):
                last = isinstance(dg, int) and dg == NG - 1
                for ct in range(CT + 1):
                    i = CT * dg + ct
                    if ct < CT:
                        if ct > 1:
                            dve.wait_ge(centred, XT * L + i - 1)
                        add_terms(G, ct, total[:, ct % 2, :], scale=pscale[:, i:i + 1] if scaled else 1.0)
                    if ct:
                        n, i = ct - 1, i - 1
                        dve.wait_ge(evacuated, 4 * G + n + 1)
                        dve.wait_ge(prepared, NG * L + dg + 1)
                        nc.vector.tensor_tensor(row(i), total[:, n % 2, :], row(i), ALU.add).then_inc(centred, 1)
                        if not last:
                            add_centred(L, i)
                            if n:
                                add_square(L, i - 1, n - 1)
                if not last:
                    add_square(L, CT * dg + CT - 1, CT - 1)

            def finish_norm(L, last=False):
                scale = FIRST / D
                dve.wait_ge(stats_multiplied, 2 * L + 2)
                step(nc.vector.tensor_scalar(shift[:, :], bank[5][:, 0:T], scale, None, ALU.mult))
                step(nc.vector.tensor_tensor(rstd[:, :], shift[:, :], shift[:, :], ALU.mult))
                nc.vector.scalar_tensor_tensor(out=variance[:, :], in0=bank[6][:, 0:T], scalar=scale,
                                               in1=rstd[:, :], op0=ALU.mult,
                                               op1=ALU.subtract).then_inc(variance_ready, 1)
                step(nc.vector.tensor_tensor(r[:, 0:2, :], r[:, 0:2, :], per_tile(shift[:, :], 2), ALU.subtract))
                dve.wait_ge(deviation_ready, L + 1)
                step(nc.vector.reciprocal(out=rstd[:, :], in_=deviation[:, :]))
                for b in range(XT // 2):
                    two = slice(2 * b, 2 * b + 2)
                    if b:
                        step(nc.vector.tensor_tensor(r[:, two, :], r[:, two, :], per_tile(shift[:, :], 2),
                                                     ALU.subtract))
                    nc.vector.tensor_tensor(r[:, two, :], r[:, two, :], per_tile(rstd[:, :], 2),
                                            ALU.mult).then_inc(normalized, 1)
                    if not last and b:
                        take_x_low(L, b - 1)
                if not last:
                    take_x_low(L, XT // 2 - 1)

            def take_x_low(L, b):
                two = slice(2 * b, 2 * b + 2)
                dve.wait_ge(x_high, NG + 8 * L + b + 1)
                nc.vector.tensor_tensor(xs[:, two, T:2 * T], r[:, two, :], xs[:, two, 0:T].bitcast(f32),
                                        ALU.subtract).then_inc(x_split, 1)

            nc.vector.memset(x_pad[:, :, 0:PAD], 0.0).then_inc(pads_zeroed, 1)
            nc.vector.memset(window_a[:, :, 0:PAD], 0.0).then_inc(pads_zeroed, 1)
            nc.vector.memset(window_b[:, :, 0:PAD], 0.0).then_inc(pads_zeroed, 1)
            dve.wait_ge(pads_zeroed, 3)
            for g, w in enumerate(WINDOWS):
                tiles = slice(CT * g, CT * g + CT)
                dve.wait_ge(x_padded, 2 * g + 2)
                summed, width, target = x_pad[:, tiles, :], 1, window_a
                while width < w:
                    step(nc.vector.tensor_tensor(target[:, :, PAD:], summed[:, :, PAD:],
                                                 summed[:, :, PAD - width:PAD + T - width], ALU.add))
                    summed, width = target[:, :, :], 2 * width
                    target = window_b if target is window_a else window_a
                if g:
                    dve.wait_ge(pool_split, g)
                step(nc.vector.scalar_tensor_tensor(out=pooled[:, :, :], in0=summed[:, :, PAD:], scalar=1.0 / w,
                                                    in1=x_pad[:, tiles, PAD:], op0=ALU.mult, op1=ALU.subtract))
                dve.wait_ge(consts_ready, 6 + PAD)
                step(nc.vector.tensor_tensor(pooled[:, :, 0:w - 1], summed[:, :, PAD:PAD + w - 1],
                                             count[:, 0:w - 1].unsqueeze(1).broadcast_to([P, CT, w - 1]), ALU.mult))
                nc.vector.tensor_tensor(pooled[:, :, 0:w - 1], pooled[:, :, 0:w - 1],
                                        x_pad[:, tiles, PAD:PAD + w - 1], ALU.subtract).then_inc(pool_ready, 1)
                dve.wait_ge(x_high, g + 1)
                step(nc.vector.tensor_tensor(xs[:, tiles, T:2 * T], x_pad[:, tiles, PAD:],
                                             xs[:, tiles, 0:T].bitcast(f32), ALU.subtract))
                if g < 2:
                    take_low(g, g)
                dve.wait_ge(pool_high, g + 1)
                nc.vector.tensor_tensor(gs[:, tiles, T:2 * T], pooled[:, :, :], gs[:, tiles, 0:T].bitcast(f32),
                                        ALU.subtract).then_inc(pool_split, 1)
            dve.wait_ge(params_copied, 4)
            prepare(0, 0)
            empty_first(0, 0, scaled=True)
            take_low(2, 2)
            centre_first(0)
            prepare(0, 1)
            empty_residual(0, 1, 1, scaled=True)
            take_low(3, 3)
            prepare(0, 2)
            empty_residual(0, 2, 2, scaled=True)
            take_low(C0["up0"], 0)
            prepare(0, 3)
            empty_residual(0, 3, 3, scaled=True)
            take_low(C0["up0"] + 1, 1)
            finish_norm(0)

            def add_taps(layer, j, half):
                tiles = group_tiles(j)
                G = G0[f"up{layer}"] + 2 * j + half
                n = 2 * UJ * CT * layer + CT * (2 * j + half)
                target = value if half else gate

                def taps(ct):
                    col = half * FT + j * CT + ct
                    dve.wait_ge(first_tap, n + ct + 1)
                    nc.vector.scalar_tensor_tensor(out=convs[:, ct % 2, :], in0=hidden[:, ct % 2, 1:1 + T],
                                                   scalar=convp[:, 4 * layer + 1, bass.ds(col, 1)],
                                                   in1=convs[:, ct % 2, :], op0=ALU.mult, op1=ALU.add
                                                   ).then_inc(middle_tap, steps_of(ct, tiles))
                    dve.wait_ge(middle_tap, n + ct + 1)
                    nc.vector.scalar_tensor_tensor(out=target[:, ct, :], in0=hidden[:, ct % 2, 0:T],
                                                   scalar=convp[:, 4 * layer, bass.ds(col, 1)],
                                                   in1=convs[:, ct % 2, :], op0=ALU.mult, op1=ALU.add
                                                   ).then_inc(convolved, steps_of(ct, tiles))

                done = (2 * UJ + 1) * CT * layer + CT + CT * (2 * j + half)
                if half == 0 and not (isinstance(j, int) and UJ * layer + j == 0):
                    dve.wait_ge(inner_split, UJ * layer + j)
                for ct in range(tiles):
                    dve.wait_ge(convolved, done + ct - 1)
                    add_terms(G, ct, hidden[:, ct % 2, 2:2 + T], tiles, banks=4 * half)
                    if ct:
                        taps(ct - 1)
                taps(tiles - 1)

            def multiply_gate(layer, j):
                tiles = group_tiles(j)
                dve.wait_ge(silu_done, UJ * layer + j + 1)
                dve.wait_ge(convolved, (2 * UJ + 1) * CT * layer + CT + CT * (2 * j + 2))
                nc.vector.tensor_tensor(value[:, 0:tiles, :], gate[:, 0:tiles, :], value[:, 0:tiles, :],
                                        ALU.mult).then_inc(products, 1)

            def take_inner_low(layer, j):
                tiles = group_tiles(j)
                part = bass.ds(j * CT, tiles)
                dve.wait_ge(inner_high, UJ * layer + j + 1)
                nc.vector.tensor_tensor(gs[:, part, T:2 * T], value[:, 0:tiles, :], gs[:, part, 0:T].bitcast(f32),
                                        ALU.subtract).then_inc(inner_split, 1)

            def up_group(layer, j, first=False):
                c0, tiles = C0[f"up{layer}"] + 2 * DC * j, group_tiles(j)
                for k in range(2 * DC):
                    if not (first and k < 2):
                        take_low(c0 + k, k, tiles=tiles)
                    if not first:
                        if k == 0:
                            add_taps(layer, j - 1, 1)
                        if k == 1:
                            multiply_gate(layer, j - 1)
                        if k == 2:
                            take_inner_low(layer, j - 1)
                    if k == 4:
                        add_taps(layer, j, 0)

            for layer in range(DEPTH):
                dve.wait_ge(x_split, 16 * layer + 8)
                nc.vector.memset(hidden[:, :, 0:2], 0.0).then_inc(convolved, CT)
                dve.wait_ge(convolved, (2 * UJ + 1) * CT * layer + CT)
                up_group(layer, 0, first=True)
                with dve.Fori(1, UJ - 1) as j:
                    up_group(layer, j)
                up_group(layer, UJ - 1)
                c0, g0, L = C0[f"down{layer}"], G0[f"down{layer}"], 2 * layer + 1

                def down_group(dg):
                    for k in range(FC):
                        take_low(c0 + FC * dg + k, k, DOWN_ROWS[k])
                        if isinstance(dg, int) and dg == 0:
                            if k == 0:
                                add_taps(layer, UJ - 1, 1)
                            if k == 1:
                                multiply_gate(layer, UJ - 1)
                            if k == 2:
                                take_inner_low(layer, UJ - 1)
                            if k == 4:
                                dve.wait_ge(inner_split, UJ * layer + UJ)
                                prepare(L, 0)
                        elif isinstance(dg, int) and dg == 1:
                            if k == 0:
                                empty_first(L, g0)
                            if k == 2:
                                centre_first(L)
                            if k == 4:
                                prepare(L, 1)
                        else:
                            if k == 0:
                                empty_residual(L, g0 + dg - 1, dg - 1)
                            if k == 4:
                                prepare(L, dg)

                down_group(0)
                down_group(1)
                with dve.Fori(2, NG) as dg:
                    down_group(dg)
                if layer == 1:
                    empty_residual(L, g0 + NG - 1, NG - 1)
                    finish_norm(L, last=True)
                    break
                take_low(C0["qkv"], 0)
                empty_residual(L, g0 + NG - 1, NG - 1)
                take_low(C0["qkv"] + 1, 1)
                finish_norm(L)

                def heads_in(g, part):
                    target = (v_t, q_t, k_t)[part]
                    for ct in range(CT):
                        add_terms(G0["qkv"] + 3 * g + part, ct, target[:, ct, :])

                def score_functions(g):
                    dve.wait_ge(z_copied, 4 * g + 4)
                    nc.vector.scalar_tensor_tensor(out=soft[:, :, :], in0=z[:, :, :], scalar=-1.0, in1=z[:, :, :],
                                                   op0=ALU.mult, op1=ALU.max).then_inc(z_abs, 1)
                    dve.wait_ge(z_log, g + 1)
                    nc.vector.scalar_tensor_tensor(out=soft[:, :, :], in0=z[:, :, :], scalar=0.0,
                                                   in1=soft[:, :, :], op0=ALU.max, op1=ALU.add).then_inc(softplus, 1)

                def weight_logs(g):
                    for h in range(CT):
                        dve.wait_ge(heads_multiplied, 16 * g + 8 + h + 1)
                        nc.vector.scalar_tensor_tensor(out=z[:, h, :], in0=bank[4 + h][:, 0:3 * P],
                                                       scalar=-float(FIRST), in1=z[:, h, :],
                                                       op0=ALU.mult, op1=ALU.add).then_inc(log_weights, 1)

                def take_heads_low(g):
                    for h in range(CT):
                        i = bass.ds(CT * g + h, 1)
                        dve.wait_ge(heads_high, 4 * g + h + 1)
                        nc.vector.tensor_tensor(gs[:, i, T:2 * T].rearrange("p o t -> p (o t)"), bank[4 + h][:, 0:T],
                                                gs[:, i, 0:T].bitcast(f32).rearrange("p o t -> p (o t)"),
                                                ALU.subtract).then_inc(heads_split, 1)

                def qkv_group(g, first=False):
                    for k in range(3 * DC):
                        if not (first and k < 2):
                            take_low(C0["qkv"] + 3 * DC * g + k, k)
                        if k == 0 and not first:
                            heads_in(g - 1, 2)
                        if k == 2 and not first:
                            score_functions(g - 1)
                        if k == 4:
                            if not first:
                                weight_logs(g - 1)
                            heads_in(g, 0)
                        if k == 6 and not first:
                            take_heads_low(g - 1)
                        if k == 8:
                            heads_in(g, 1)

                qkv_group(0, first=True)
                with dve.Fori(1, NG) as g:
                    qkv_group(g)

                def attn_out_group(dg):
                    for k in range(DC):
                        take_low(C0["attn_out"] + DC * dg + k, k)
                        if isinstance(dg, int) and dg == 0:
                            if k == 0:
                                heads_in(NG - 1, 2)
                            if k == 1:
                                prepare(2, 0)
                            if k == 2:
                                score_functions(NG - 1)
                                weight_logs(NG - 1)
                                take_heads_low(NG - 1)
                        elif isinstance(dg, int) and dg == 1:
                            if k == 0:
                                empty_first(2, G0["attn_out"])
                            if k == 2:
                                centre_first(2)
                                prepare(2, 1)
                        else:
                            if k == 0:
                                empty_residual(2, G0["attn_out"] + dg - 1, dg - 1)
                            if k == 2:
                                prepare(2, dg)

                attn_out_group(0)
                attn_out_group(1)
                with dve.Fori(2, NG) as dg:
                    attn_out_group(dg)
                take_low(C0["up1"], 0)
                empty_residual(2, G0["attn_out"] + NG - 1, NG - 1)
                take_low(C0["up1"] + 1, 1)
                finish_norm(2)

            for n in range(2 * NG):
                dq, tt = n // 2, n % 2
                dve.wait_ge(out_transposed, n + 1)
                nc.vector.tensor_copy(o_sb[:, tt, dq * WC:(dq + 1) * WC], bank[n][:, :]).then_inc(out_copied, 1)

        @block.tensor
        def _(pe):
            def multiply(c, k, rhs, rows, tiles=CT, banks=0, first=False, last=False, before=None, slot=None):
                slot = k % 2 if slot is None else slot
                for ct in range(tiles):
                    if ct % 2 == 0:
                        pe.wait_ge(weights_split, 2 * c + ct // 2 + 1)
                    if before is not None:
                        pe.wait_ge(evacuated, 4 * before + ct + 1)
                    for kk in range(rows):
                        w = (slice(None), kk, slice(ct * P, ct * P + P))
                        nc.tensor.matmul(bank[banks + ct][:, :], high[slot][w], rhs[kk],
                                         start=first and kk == 0, stop=False)
                        op = nc.tensor.matmul(bank[banks + ct][:, T:2 * T], low[slot][w], rhs[kk][:, 0:T],
                                              start=False, stop=last and kk == rows - 1)
                    op.then_inc(tiles_multiplied, steps_of(ct, tiles))

            def find_centre(L):
                pe.wait_ge(part_summed, L + 1)
                nc.tensor.matmul(bank[4][:, 0:T], mean_w[:, :], sum_c[:, :], start=True,
                                 stop=True).then_inc(centre_multiplied, 1)

            def statistics(L):
                pe.wait_ge(sums_c, 12 * L + 12)
                nc.tensor.matmul(bank[5][:, 0:T], mean_w[:, :], sum_c[:, :], start=True, stop=False)
                pe.wait_ge(sums_q, 12 * L + 12)
                nc.tensor.matmul(bank[6][:, 0:T], mean_w[:, :], sum_q[:, :], start=True, stop=False)
                for i in range(XT - CT, XT):
                    end = i == XT - 1
                    pe.wait_ge(centred, XT * L + i + 1)
                    one = nc.tensor.matmul(bank[5][:, 0:T], mean_w[:, :], r[:, i, :], start=False, stop=end)
                    if end:
                        one.then_inc(stats_multiplied, 1)
                    pe.wait_ge(squared, XT * L + i + 1)
                    two = nc.tensor.matmul(bank[6][:, 0:T], mean_w[:, :], squares[:, i % 4, :], start=False, stop=end)
                    if end:
                        two.then_inc(stats_multiplied, 1)

            pe.wait_ge(consts_ready, 6 + PAD)
            pe.wait_ge(x_loaded, 16)
            for i in range(XT):
                for tt in range(TT):
                    at_col = (i % 2) * T + tt * P
                    op = nc.tensor.transpose(bank[i // 2][:, at_col:at_col + P], x_in[:, tt, i * P:(i + 1) * P],
                                             ident[:, :])
                if i % 2:
                    op.then_inc(x_transposed, 1)
            pe.wait_ge(params_loaded, 16 * (4 * DEPTH + 4 + 1))
            pe.wait_ge(x_padded, 4)
            for layer in range(DEPTH):
                for n in range(4):
                    op = nc.tensor.transpose(bank[layer][:, n * 2 * FT:(n + 1) * 2 * FT],
                                             conv_in[:, 4 * layer + n, :], ident[0:2 * FT, 0:2 * FT])
                op.then_inc(params_transposed, 1)
            nc.tensor.transpose(bank[2][:, 0:P], ln_in[:, :], ident[:, :]).then_inc(params_transposed, 1)
            nc.tensor.transpose(bank[3][:, 0:XT], pscale_in[:, :], ident[0:XT, 0:XT]).then_inc(params_transposed, 1)
            pe.wait_ge(params_copied, 4)
            pe.wait_ge(x_padded, 8)
            for g in range(NG):
                pe.wait_ge(pool_split, g + 1)
                multiply(g, g, [gs[:, CT * g + kk, :] for kk in range(KT)], KT, first=True, last=True,
                         before=g - 1 if g else None)
                if g == 1:
                    find_centre(0)
            statistics(0)

            for layer in range(DEPTH):
                def up_group(j):
                    tiles = group_tiles(j)
                    for half in range(2):
                        for k in range(DC):
                            pe.wait_ge(x_split, 8 * (2 * layer) + 2 * (k + 1))
                            G = G0[f"up{layer}"] + 2 * j + half
                            multiply(C0[f"up{layer}"] + 2 * DC * j + DC * half + k, k,
                                     [xs[:, k * KT + kk, :] for kk in range(KT)], KT, tiles, 4 * half,
                                     first=k == 0, last=k == DC - 1, before=G - 2 if k == 0 else None)

                with pe.Fori(0, UJ - 1) as j:
                    up_group(j)
                up_group(UJ - 1)

                c0, g0, L = C0[f"down{layer}"], G0[f"down{layer}"], 2 * layer + 1

                def down_group(dg):
                    for k in range(FC):
                        start, rows = sum(DOWN_ROWS[:k]), DOWN_ROWS[k]
                        pe.wait_ge(inner_split, UJ * layer + (start + rows - 1) // CT + 1)
                        before = (g0 - 2 if isinstance(dg, int) and dg == 0 else g0 + dg - 1) if k == 0 else None
                        multiply(c0 + FC * dg + k, k, [gs[:, start + kk, :] for kk in range(rows)], rows,
                                 first=k == 0, last=k == FC - 1, before=before)
                        if isinstance(dg, int) and dg == 1 and k == 0:
                            find_centre(L)

                down_group(0)
                down_group(1)
                with pe.Fori(2, NG) as dg:
                    down_group(dg)
                statistics(L)
                if layer == 1:
                    break

                def transpose_values(g):
                    if isinstance(g, int) and g == 0:
                        pe.wait_ge(evacuated, 4 * G0["qkv"] + 4)
                    else:
                        pe.wait_ge(evacuated, 4 * (G0["qkv"] + 3 * g) + 4)
                        pe.wait_ge(heads_split, 4 * g)
                    for h in range(CT):
                        for kt in range(TT):
                            op = nc.tensor.transpose(bank[4 + h][:, kt * P:(kt + 1) * P],
                                                     v_t[:, h, kt * P:(kt + 1) * P], ident[:, :])
                        op.then_inc(heads_multiplied, 1)

                def scores(g):
                    pe.wait_ge(evacuated, 4 * (G0["qkv"] + 3 * g + 2) + 4)
                    for h in range(CT):
                        pe.wait_ge(v_copied, 4 * g + h + 1)
                        nc.tensor.matmul(bank[4 + h][:, 0:T], k_t[:, h, 0:P], q_t[:, h, :], start=True, stop=False)
                        nc.tensor.matmul(bank[4 + h][:, T:T + P], k_t[:, h, P:T], q_t[:, h, P:T], start=False,
                                         stop=True).then_inc(heads_multiplied, 1)

                def sum_softplus(g):
                    pe.wait_ge(masked, 4 * g + 2)
                    for h in range(CT):
                        pe.wait_ge(z_copied, 4 * g + h + 1)
                        nc.tensor.matmul(bank[4 + h][:, 0:T], tri_w[:, :], soft[:, h, 0:T], start=True, stop=False)
                        nc.tensor.matmul(bank[4 + h][:, T:T + P], tri_w[:, :], soft[:, h, T:T + P], start=False,
                                         stop=False)
                        nc.tensor.matmul(bank[4 + h][:, P:T], mean_w[:, :], soft[:, h, T:T + P], start=False,
                                         stop=True).then_inc(heads_multiplied, 1)

                def weigh_values(g):
                    pe.wait_ge(masked, 4 * g + 4)
                    for h in range(CT):
                        nc.tensor.matmul(bank[4 + h][:, 0:T], v_n[:, h, 0:P], z[:, h, 0:T], start=True, stop=False)
                        nc.tensor.matmul(bank[4 + h][:, P:T], v_n[:, h, P:T], z[:, h, T:T + P], start=False,
                                         stop=True).then_inc(heads_multiplied, 1)

                def qkv_group(g, first=False):
                    for k in range(3 * DC):
                        part, n = k // DC, k % DC
                        pe.wait_ge(x_split, 8 + 2 * (n + 1))
                        G = G0["qkv"] + 3 * g + part
                        multiply(C0["qkv"] + 3 * DC * g + k, k, [xs[:, n * KT + kk, :] for kk in range(KT)], KT,
                                 first=n == 0, last=n == DC - 1, before=G - 1 if n == 0 else None)
                        if not first:
                            if k == 0:
                                scores(g - 1)
                            if k == 2:
                                sum_softplus(g - 1)
                            if k == 4:
                                weigh_values(g - 1)
                        if k == 6:
                            transpose_values(g)

                qkv_group(0, first=True)
                with pe.Fori(1, NG) as g:
                    qkv_group(g)

                def attn_out_group(dg):
                    for k in range(DC):
                        pe.wait_ge(heads_split, 4 * k + 4)
                        G = G0["attn_out"] + dg
                        multiply(C0["attn_out"] + DC * dg + k, k, [gs[:, k * KT + kk, :] for kk in range(KT)], KT,
                                 first=k == 0, last=k == DC - 1, before=G - 1 if k == 0 else None)
                        if isinstance(dg, int) and dg == 0:
                            if k == 0:
                                scores(NG - 1)
                            if k == 1:
                                sum_softplus(NG - 1)
                            if k == 2:
                                weigh_values(NG - 1)
                        if isinstance(dg, int) and dg == 1 and k == 0:
                            find_centre(2)

                attn_out_group(0)
                attn_out_group(1)
                with pe.Fori(2, NG) as dg:
                    attn_out_group(dg)
                statistics(2)

            for n in range(2 * NG):
                dq, tt = n // 2, n % 2
                pe.wait_ge(affine, XT * 3 + CT * dq + CT)
                if n == 0:
                    pe.wait_ge(evacuated, 4 * G0["end"])
                if n == 5:
                    pe.wait_ge(variance_ready, 4)
                for q in range(CT):
                    op = nc.tensor.transpose(bank[n][:, q * P:(q + 1) * P],
                                             r[:, CT * dq + q, tt * P:(tt + 1) * P], ident[:, :])
                op.then_inc(out_transposed, 1)


INPUTS = ["x", "pool_w", "pool_scale", "attn_w_qkv", "attn_w_o", "ffn_w_up", "ffn_conv_w", "ffn_conv_b",
          "ffn_w_down", "ln_mix_g", "ln_mix_b", "ln_ffn_g", "ln_ffn_b"]


def kernel(**inputs):
    import numpy as np
    import concourse.bacc as bacc
    from concourse.bass_utils import run_bass_kernel_spmd

    nc = bacc.Bacc("TRN2", target_bir_lowering=False, num_devices=1, dynamic_dma_scratch_size=4096)
    arrays, args = {}, []
    for name in INPUTS:
        a = np.ascontiguousarray(inputs[name])
        arrays[f"in_{name}"] = a
        args.append(nc.dram_tensor(f"in_{name}", a.shape, mybir.dt.from_np(a.dtype), kind="ExternalInput").ap())
    shape = inputs["x"].shape
    out = nc.dram_tensor("out_x", shape, mybir.dt.float32, kind="ExternalOutput").ap()
    decoder_trunk(nc, *args, out)
    result = run_bass_kernel_spmd(nc, [arrays], core_ids=[0])
    return result.results[0]["out_x"]
```

```python
import concourse.bass as bass
from concourse import mybir
from contextlib import ExitStack


def decoder_trunk(nc, x, pool_w, pool_scale, attn_w_qkv, attn_w_o, ffn_w_up, ffn_conv_w, ffn_conv_b,
                  ffn_w_down, ln_mix_g, ln_mix_b, ln_ffn_g, ln_ffn_b, out):
    f32 = mybir.dt.float32
    f32r = mybir.dt.float32r
    ALU = mybir.AluOpType
    ACT = mybir.ActivationFunctionType
    AX = mybir.AxisListType

    P = 128
    T = x.shape[1]
    D = x.shape[2]
    DEPTH = ffn_w_up.shape[0]
    FF = ffn_w_down.shape[1]
    TT = T // P
    XT = D // P
    FT = FF // P
    CT = 4
    KT = 4
    WC = CT * P
    NG = XT // CT
    TAPS = ffn_conv_w.shape[1]
    ALPHA = float((2.0 * DEPTH) ** 0.25)
    EPS = 1e-5
    ZSCALE = float(P) ** -0.5
    WINDOWS = (2, 4, 8, 16)
    PAD = WINDOWS[-1]
    FIRST = CT * P
    assert (T, TT, XT, NG, TAPS, DEPTH) == (2 * P, 2, 16, 4, 3, 2) and FF == FT * P

    UJ = -(-FT // CT)
    LAST_TILES = FT - (UJ - 1) * CT
    D_ROWS = [KT] * (XT // KT)
    DOWN_ROWS = [3, 3, 3, 2] + [4] * 8
    assert sum(DOWN_ROWS) == FT and len(DOWN_ROWS) % 4 == 0
    DC, FC = len(D_ROWS), len(DOWN_ROWS)

    names = ["pool", "up0", "down0", "qkv", "attn_out", "up1", "down1", "end"]
    chunks = [NG, 2 * UJ * DC, NG * FC, 3 * NG * DC, NG * DC, 2 * UJ * DC, NG * FC]
    groups = [NG, 2 * UJ, NG, 3 * NG, NG, 2 * UJ, NG]
    C0 = {n: sum(chunks[:i]) for i, n in enumerate(names)}
    G0 = {n: sum(groups[:i]) for i, n in enumerate(names)}
    assert all(c % 4 == 0 for c in C0.values())

    ctx = ExitStack()
    with ctx:
        top = [-(-nc.sbuf_base // 64) * 64]

        def at(name, shape, dtype, offset):
            return nc.alloc_sbuf_tensor_at(name, shape, dtype, offset=offset)

        def place(name, shape, dtype):
            size = 4
            for n in shape[1:]:
                size *= n
            t = at(name, shape, dtype, top[0])
            top[0] += -(-size // 64) * 64
            return t

        raw = [place(f"raw{i}", [P, KT, WC], f32) for i in range(4)]
        high = [place(f"weights_high{i}", [P, KT, WC], f32r) for i in range(2)]
        low = [place(f"weights_low{i}", [P, KT, WC], f32r) for i in range(2)]
        xs = place("xs", [P, XT, 2 * T], f32r)
        r_at = top[0]
        r = place("r", [P, XT, T], f32)
        gs_at = top[0]
        gs = place("gs", [P, FT, 2 * T], f32r)
        cross = place("cross", [P, 2, T], f32)
        total = place("total", [P, 2, T], f32)
        centre = place("centre", [P, T], f32)
        sum_c = place("sum_c", [P, T], f32)
        sum_q = place("sum_q", [P, T], f32)
        squares = place("squares", [P, 4, T], f32)
        shift = place("shift", [P, T], f32)
        variance = place("variance", [P, T], f32)
        deviation = place("deviation", [P, T], f32)
        rstd = place("rstd", [P, T], f32)
        ident = place("ident", [P, P], f32)
        mean_w = place("mean_w", [P, P], f32)
        tri_w = place("tri_w", [P, P], f32)
        convp = place("convp", [P, 4 * DEPTH, 2 * FT], f32)
        lnp = place("lnp", [P, 4, DEPTH, XT], f32)
        pscale = place("pscale", [P, XT], f32)
        count = place("count", [P, PAD], f32)
        eps = place("eps", [P, 1], f32)
        assert top[0] <= nc.sbuf_usable_end

        hidden = at("hidden", [P, 2, T + 2], f32, r_at)
        convs = at("convs", [P, 2, T], f32, r_at + 2112)
        gate = at("gate", [P, CT, T], f32, r_at + 4160)
        value = at("value", [P, CT, T], f32, r_at + 8256)
        free = gs_at + XT * 2 * T * 4
        x_in = at("x_in", [P, TT, D], f32, free)
        band = at("band", [P, NG, 2, P], f32, free + 16384)
        corner = at("corner", [P, NG, PAD], f32, free + 20480)
        conv_in = at("conv_in", [2 * FT, 4 * DEPTH, P], f32, free + 46592)
        ln_in = at("ln_in", [P, P], f32, free + 50688)
        pscale_in = at("pscale_in", [XT, P], f32, free + 51200)
        v_t = at("v_t", [P, CT, T], f32, free)
        q_t = at("q_t", [P, CT, T], f32, free + 4096)
        k_t = at("k_t", [P, CT, T], f32, free + 8192)
        v_n = at("v_n", [P, CT, T], f32, free + 12288)
        z = at("z", [P, CT, 3 * P], f32, free + 16384)
        soft = at("soft", [P, CT, 3 * P], f32, free + 22528)
        o_sb = at("o_sb", [P, TT, D], f32, gs_at)

        bank = [ctx.enter_context(nc.psum_tensor(f"bank{i}", [P, WC], f32)) for i in range(8)]

        def sem(name):
            return ctx.enter_context(nc.semaphore(name))

        weights_loaded = [sem(f"weights_loaded{i}") for i in range(4)]
        weights_high = sem("weights_high_ready")
        weights_split = sem("weights_split")
        tiles_multiplied = sem("tiles_multiplied")
        cross_copied = sem("cross_copied")
        evacuated = sem("evacuated")
        x_loaded = [sem(f"x_loaded{g}") for g in range(NG)]
        params_loaded, conv_loaded = sem("params_loaded"), sem("conv_loaded")
        consts_ready = sem("consts_ready")
        band_filled, band_cut, band_ready = sem("band_filled"), sem("band_cut"), sem("band_ready")
        x_transposed, x_copied = sem("x_transposed"), sem("x_copied")
        params_transposed, params_copied = sem("params_transposed"), sem("params_copied")
        pool_multiplied, pool_high, pool_split = (
            sem("pool_multiplied"), sem("pool_high"), sem("pool_split"))
        part_summed = sem("part_summed")
        centre_multiplied, centre_copied = sem("centre_multiplied"), sem("centre_copied")
        half_prepared, prepared = sem("half_prepared"), sem("prepared")
        centred = sem("centred")
        squared = sem("squared")
        sums_c, sums_q = sem("sums_c"), sem("sums_q")
        stats_multiplied = sem("stats_multiplied")
        variance_ready, deviation_ready = sem("variance_ready"), sem("deviation_ready")
        normalized = sem("normalized")
        affine = sem("affine")
        x_high, x_split = sem("x_high"), sem("x_split")
        first_tap, middle_tap, convolved = sem("first_tap"), sem("middle_tap"), sem("convolved")
        silu_done, products, inner_high, inner_split = (
            sem("silu_done"), sem("products"), sem("inner_high"), sem("inner_split"))
        heads_multiplied = sem("heads_multiplied")
        v_copied, z_copied = sem("v_copied"), sem("z_copied")
        z_abs, z_exp, z_log, softplus = sem("z_abs"), sem("z_exp"), sem("z_log"), sem("softplus")
        masked = sem("masked")
        log_weights, weights_exp = sem("log_weights"), sem("weights_exp")
        heads_high, heads_split = sem("heads_high"), sem("heads_split")
        out_transposed, out_copied, out_stored = sem("out_transposed"), sem("out_copied"), sem("out_stored")
        vector_steps = sem("vector_steps")

        block = ctx.enter_context(nc.Block())

        def halves(tiles):
            return (slice(0, 2 * P), slice(2 * P, tiles * P))

        def group_tiles(j):
            return LAST_TILES if isinstance(j, int) and j == UJ - 1 else CT

        def steps_of(ct, tiles):
            return CT - ct if ct == tiles - 1 else 1

        @block.sync
        def _(sp):

            def load(c0, k, matrix, row_tile, rows, col, tiles=CT):
                c = c0 + k
                if not (isinstance(c, int) and c < 4):
                    sp.wait_ge(weights_split, 2 * (c - 4) + 2)
                source = matrix[row_tile * P:(row_tile + rows) * P, bass.ds(col, tiles * P)]
                sp.dma_start(raw[k % 4][:, 0:rows, 0:tiles * P],
                             source.rearrange("(t p) n -> p t n", p=P)).then_inc(weights_loaded[k % 4], 16)

            def load_up(layer, c0, j):
                for k in range(2 * DC):
                    half = k // DC
                    load(c0 + 2 * DC * j, k, ffn_w_up[layer], (k % DC) * KT, KT,
                         half * FF + j * WC, group_tiles(j))

            def load_down(layer, c0):
                with sp.Fori(0, NG) as dg:
                    for k in range(FC):
                        load(c0 + FC * dg, k, ffn_w_down[layer], sum(DOWN_ROWS[:k]), DOWN_ROWS[k], dg * WC)

            for g in range(NG):
                sp.dma_start(x_in[:, :, g * WC:(g + 1) * WC],
                             x[0, :, g * WC:(g + 1) * WC].rearrange("(t p) d -> p t d", p=P)
                             ).then_inc(x_loaded[g], 16)
                load(0, g, pool_w[0, g], 0, KT, 0)
            for layer in range(DEPTH):
                up = C0[f"up{layer}"]
                with sp.Fori(0, UJ - 1) as j:
                    load_up(layer, up, j)
                load_up(layer, up, UJ - 1)
                load_down(layer, C0[f"down{layer}"])
                if layer == 0:
                    qkv = attn_w_qkv[0].rearrange("k (s n) -> s k n", s=3)
                    with sp.Fori(1, NG + 1) as g:
                        for n, part in enumerate((2, 0, 1)):
                            for k in range(DC):
                                load(C0["qkv"] + 3 * DC * g - 3 * DC, n * DC + k, qkv[part], k * KT, KT,
                                     g * WC - WC)
                    with sp.Fori(0, NG) as dg:
                        for k in range(DC):
                            load(C0["attn_out"] + DC * dg, k, attn_w_o[0], k * KT, KT, dg * WC)
            for n in range(2 * NG):
                dq, tt = n // 2, n % 2
                sp.wait_ge(out_copied, n + 1)
                sp.dma_start(out[0, tt * P:(tt + 1) * P, dq * WC:(dq + 1) * WC],
                             o_sb[:, tt, dq * WC:(dq + 1) * WC]).then_inc(out_stored, 16)
            sp.wait_ge(out_stored, 16 * 2 * NG)

        @block.gpsimd
        def _(pool):
            nc.gpsimd.memset(ident[:, :], 0.0).then_inc(consts_ready, 1)
            pool.wait_ge(consts_ready, 1)
            nc.gpsimd.affine_select(out=ident[:, :], in_=ident[:, :], compare_op=ALU.not_equal, fill=1.0,
                                    base=0, pattern=[[-1, P]], channel_multiplier=1).then_inc(consts_ready, 1)
            for g, w in enumerate(WINDOWS):
                pool.wait_ge(band_filled, 3 * g + 3)
                both = band[:, g, :, :]
                nc.gpsimd.affine_select(out=both, in_=both, compare_op=ALU.is_ge, fill=0.0, base=0,
                                        pattern=[[0, 2], [1, P]], channel_multiplier=-1).then_inc(band_cut, 1)
                pool.wait_ge(band_cut, 3 * g + 1)
                nc.gpsimd.affine_select(out=both, in_=both, compare_op=ALU.is_ge, fill=0.0, base=w - 1,
                                        pattern=[[0, 2], [-1, P]], channel_multiplier=1).then_inc(band_cut, 1)
                nc.gpsimd.affine_select(out=corner[:, g, :], in_=corner[:, g, :], compare_op=ALU.is_ge, fill=0.0,
                                        base=w - 1 - P, pattern=[[-1, PAD]],
                                        channel_multiplier=1).then_inc(band_cut, 1)
            nc.gpsimd.memset(mean_w[:, :], 1.0 / FIRST).then_inc(consts_ready, 1)
            nc.gpsimd.memset(tri_w[:, :], 1.0 / FIRST).then_inc(consts_ready, 1)
            nc.gpsimd.memset(eps[:, :], EPS).then_inc(consts_ready, 1)
            pool.wait_ge(consts_ready, 5)
            nc.gpsimd.affine_select(out=tri_w[:, :], in_=tri_w[:, :], compare_op=ALU.is_ge, fill=0.0,
                                    base=0, pattern=[[-1, P]], channel_multiplier=1).then_inc(consts_ready, 1)

            def add_sums(i):
                pool.wait_ge(squared, i + 1)
                pool.wait_ge(sums_q, i)
                nc.gpsimd.tensor_tensor(sum_q[:, :], sum_q[:, :], squares[:, i % CT, :], ALU.add).then_inc(sums_q, 1)
                if i >= CT:
                    pool.wait_ge(centred, i + 1)
                    pool.wait_ge(sums_c, i)
                    nc.gpsimd.tensor_tensor(sum_c[:, :], sum_c[:, :], r[:, i, :], ALU.add).then_inc(sums_c, 1)

            pool.wait_ge(squared, 2)
            nc.gpsimd.tensor_tensor(sum_q[:, :], squares[:, 0, :], squares[:, 1, :], ALU.add).then_inc(sums_q, 2)
            for i in range(2, XT - CT):
                add_sums(i)

            def mask(tile, block_at):
                part = tile[:, :, block_at * P:(block_at + 1) * P]
                nc.gpsimd.affine_select(out=part, in_=part, compare_op=ALU.is_gt, fill=0.0, base=0,
                                        pattern=[[0, CT], [1, P]], channel_multiplier=-1).then_inc(masked, 1)

            for g in range(NG):
                pool.wait_ge(softplus, g + 1)
                mask(soft, 0)
                mask(soft, 2)
                pool.wait_ge(weights_exp, g + 1)
                mask(z, 0)
                mask(z, 2)

        @block.scalar
        def _(act):
            act.dma_start(pscale_in[:, :], pool_scale[0].rearrange("(t p) -> t p", p=P)).then_inc(params_loaded, 16)
            for n, source in enumerate((ln_mix_g, ln_mix_b, ln_ffn_g, ln_ffn_b)):
                act.dma_start(ln_in[n * DEPTH * XT:(n + 1) * DEPTH * XT, :],
                              source.rearrange("l (t p) -> (l t) p", p=P)).then_inc(params_loaded, 16)
            for layer in range(DEPTH):
                for n, source in enumerate([ffn_conv_w[layer, i] for i in range(TAPS)] + [ffn_conv_b[layer]]):
                    act.dma_start(conv_in[:, 4 * layer + n, :],
                                  source.rearrange("(t p) -> t p", p=P)).then_inc(conv_loaded, 16)

            def take_high(c0, k, rows=KT, tiles=CT, which=(0, 1)):
                c = c0 + k
                if 0 in which:
                    act.wait_ge(weights_loaded[k % 4], 4 * c0 + 16 * (k // 4 + 1))
                for h in which:
                    cols = halves(tiles)[h]
                    if not (isinstance(c, int) and c < 2):
                        act.wait_ge(tiles_multiplied, 4 * (c - 2) + 2 * h + 2)
                    nc.scalar.activation(high[k % 2][:, 0:rows, cols], raw[k % 4][:, 0:rows, cols],
                                         ACT.Copy).then_inc(weights_high, 1)

            def copy_cross(G, c_end, ct, tiles=CT, banks=0, scale=None):
                act.wait_ge(tiles_multiplied, 4 * c_end + ct + 1)
                if not (isinstance(G, int) and G == 0 and ct < 2):
                    act.wait_ge(evacuated, 4 * G + ct - 1)
                source = bank[banks + ct][:, T:2 * T]
                if scale is None:
                    op = nc.scalar.activation(cross[:, ct % 2, :], source, ACT.Copy)
                else:
                    op = nc.scalar.activation(cross[:, ct % 2, :], source, ACT.Identity, scale=scale)
                op.then_inc(cross_copied, steps_of(ct, tiles))

            def squares_of(L, dg, ct):
                i = CT * dg + ct
                act.wait_ge(centred, XT * L + i + 1)
                if not (isinstance(dg, int) and dg == 0):
                    act.wait_ge(sums_q, 12 * L + i - 3)
                nc.scalar.activation(squares[:, ct, :], r[:, bass.ds(i, 1), :].rearrange("p o t -> p (o t)"),
                                     ACT.Square).then_inc(squared, 1)

            def empty_residual(L, G, dg, c_end, scaled=False, between=None):
                for ct in range(CT):
                    i = CT * dg + ct
                    copy_cross(G, c_end, ct, scale=pscale[:, i:i + 1] if scaled else None)
                    if ct and not (isinstance(dg, int) and dg == 0):
                        squares_of(L, dg, ct - 1)
                    if ct == 2 and between:
                        between()
                if not (isinstance(dg, int) and dg == 0):
                    squares_of(L, dg, CT - 1)

            def copy_centre(L):
                act.wait_ge(centre_multiplied, L + 1)
                nc.scalar.activation(centre[:, :], bank[4][:, 0:T], ACT.Copy).then_inc(centre_copied, 1)
                for ct in range(CT):
                    squares_of(L, 0, ct)

            def finish_norm(L, last=False, after=None):
                which, layer = (0 if L % 2 == 0 else 2), L // 2
                if after is not None:
                    after()
                act.wait_ge(variance_ready, L + 1)
                nc.scalar.activation(deviation[:, :], variance[:, :], ACT.Sqrt, bias=eps[:, :]).then_inc(deviation_ready, 1)
                for b in range(XT // 2):
                    act.wait_ge(normalized, 8 * L + b + 1)
                    for i in (2 * b, 2 * b + 1):
                        nc.scalar.activation(r[:, i, :], r[:, i, :], ACT.Identity,
                                             scale=lnp[:, which, layer, i:i + 1],
                                             bias=lnp[:, which + 1, layer, i:i + 1]).then_inc(affine, 1)
                    if not last:
                        act.wait_ge(affine, XT * L + 2 * b + 2)
                        nc.scalar.activation(xs[:, 2 * b:2 * b + 2, 0:T], r[:, 2 * b:2 * b + 2, :],
                                             ACT.Copy).then_inc(x_high, 1)

            def pairs(b):
                return bank[b][:, :].rearrange("p (i t) -> p i t", i=2)

            def pooled_high(g):
                for n in range(2):
                    act.wait_ge(pool_multiplied, 2 * g + n + 1)
                    nc.scalar.activation(gs[:, CT * g + 2 * n:CT * g + 2 * n + 2, 0:T],
                                         pairs(4 + 2 * (g % 2) + n), ACT.Copy).then_inc(pool_high, 1)

            def copy_input(g):
                for n in (2 * g, 2 * g + 1):
                    two = slice(2 * n, 2 * n + 2)
                    act.wait_ge(x_transposed, n + 1)
                    nc.scalar.activation(r[:, two, :], pairs(n), ACT.Copy).then_inc(x_copied, 1)

            def copy_taps(layer, b):
                act.wait_ge(params_transposed, 3 + layer)
                nc.scalar.activation(convp[:, 4 * layer:4 * layer + 4, :],
                                     bank[b][:, 0:4 * 2 * FT].rearrange("p (n t) -> p n t", n=4),
                                     ACT.Copy).then_inc(params_copied, 1)

            pooled_high(0)
            copy_input(0)
            act.wait_ge(params_transposed, 1)
            nc.scalar.activation(pscale[:, :], bank[2][:, 0:XT], ACT.Copy).then_inc(params_copied, 1)
            act.wait_ge(params_transposed, 2)
            nc.scalar.activation(lnp[:, :, :, :], bank[3][:, 0:P].rearrange("p (n l t) -> p n l t", n=4, l=DEPTH),
                                 ACT.Copy).then_inc(params_copied, 1)
            pooled_high(1)
            take_high(0, 0)
            copy_input(1)
            pooled_high(2)
            take_high(0, 1)
            pooled_high(3)
            act.wait_ge(params_copied, 2)
            empty_residual(0, 0, 0, 0, scaled=True)
            copy_input(2)
            take_high(0, 2)
            copy_input(3)
            copy_centre(0)
            empty_residual(0, 1, 1, 1, scaled=True)
            take_high(0, 3)
            copy_taps(0, 7)
            empty_residual(0, 2, 2, 2, scaled=True)
            take_high(C0["up0"], 0)
            copy_taps(1, 4)
            empty_residual(0, 3, 3, 3, scaled=True, between=lambda: take_high(C0["up0"], 1, which=(0,)))
            finish_norm(0, after=lambda: take_high(C0["up0"], 1, which=(1,)))

            def up_cross(layer, j, half, between):
                tiles = group_tiles(j)
                G = G0[f"up{layer}"] + 2 * j + half
                c_end = C0[f"up{layer}"] + 2 * DC * j + DC * (half + 1) - 1
                n = (2 * UJ + 1) * CT * layer + CT + CT * (2 * j + half)

                def tap(ct):
                    col = half * FT + j * CT + ct
                    act.wait_ge(evacuated, 4 * G + ct + 1)
                    act.wait_ge(convolved, n + ct - 1)
                    nc.scalar.activation(convs[:, ct % 2, :], hidden[:, ct % 2, 2:2 + T], ACT.Identity,
                                         scale=convp[:, 4 * layer + 2, bass.ds(col, 1)],
                                         bias=convp[:, 4 * layer + 3, bass.ds(col, 1)]
                                         ).then_inc(first_tap, steps_of(ct, tiles))

                for ct in range(tiles):
                    copy_cross(G, c_end, ct, tiles, banks=4 * half)
                    if ct:
                        tap(ct - 1)
                    if ct == 2:
                        between()
                tap(tiles - 1)

            def apply_silu(layer, j):
                tiles = group_tiles(j)
                act.wait_ge(convolved, (2 * UJ + 1) * CT * layer + CT + CT * (2 * j + 1))
                nc.scalar.activation(gate[:, 0:tiles, :], gate[:, 0:tiles, :], ACT.Silu).then_inc(silu_done, 1)

            def take_inner_high(layer, j):
                tiles = group_tiles(j)
                act.wait_ge(products, UJ * layer + j + 1)
                nc.scalar.activation(gs[:, bass.ds(j * CT, tiles), 0:T], value[:, 0:tiles, :],
                                     ACT.Copy).then_inc(inner_high, 1)

            def up_group(layer, j, first=False):
                c0, tiles = C0[f"up{layer}"] + 2 * DC * j, group_tiles(j)
                for k in range(2 * DC):
                    if k in (1, 5):
                        if not (first and k == 1):
                            take_high(c0, k, tiles=tiles, which=(1,))
                    elif not (first and k == 0):
                        take_high(c0, k, tiles=tiles)
                    if k == 0 and not first:
                        up_cross(layer, j - 1, 1, lambda: take_high(c0, 1, tiles=tiles, which=(0,)))
                    if k == 2 and not first:
                        take_inner_high(layer, j - 1)
                    if k == 4:
                        up_cross(layer, j, 0, lambda: take_high(c0, 5, tiles=tiles, which=(0,)))
                    if k == 5:
                        apply_silu(layer, j)

            for layer in range(DEPTH):
                up_group(layer, 0, first=True)
                with act.Fori(1, UJ - 1) as j:
                    up_group(layer, j)
                up_group(layer, UJ - 1)
                c0, g0, L = C0[f"down{layer}"], G0[f"down{layer}"], 2 * layer + 1

                def down_group(dg):
                    def half_a():
                        take_high(c0 + FC * dg, 1, DOWN_ROWS[1], which=(0,))

                    for k in range(FC):
                        take_high(c0 + FC * dg, k, DOWN_ROWS[k], which=(1,) if k == 1 else (0, 1))
                        if isinstance(dg, int) and dg == 0:
                            if k == 0:
                                up_cross(layer, UJ - 1, 1, half_a)
                            if k == 2:
                                take_inner_high(layer, UJ - 1)
                        elif k == 0:
                            empty_residual(L, g0 + dg - 1, dg - 1, c0 + FC * dg - 1, between=half_a)
                        if isinstance(dg, int) and dg == 1 and k == 2:
                            copy_centre(L)

                down_group(0)
                down_group(1)
                with act.Fori(2, NG) as dg:
                    down_group(dg)
                if layer == 1:
                    empty_residual(L, g0 + NG - 1, NG - 1, c0 + FC * NG - 1)
                    finish_norm(L, last=True)
                    break
                take_high(C0["qkv"], 0)
                empty_residual(L, g0 + NG - 1, NG - 1, c0 + FC * NG - 1,
                               between=lambda: take_high(C0["qkv"], 1, which=(0,)))
                finish_norm(L, after=lambda: take_high(C0["qkv"], 1, which=(1,)))

                def cross_of(g, part):
                    for ct in range(CT):
                        copy_cross(G0["qkv"] + 3 * g + part, C0["qkv"] + 3 * DC * g + DC * (part + 1) - 1, ct)

                def score_functions(g):
                    for h in range(CT):
                        act.wait_ge(heads_multiplied, 16 * g + 4 + h + 1)
                        nc.scalar.activation(z[:, h, :], bank[4 + h][:, 0:3 * P], ACT.Copy,
                                             scale=ZSCALE).then_inc(z_copied, 1)
                        nc.scalar.activation(soft[:, h, :], bank[4 + h][:, 0:3 * P], ACT.Abs,
                                             scale=ZSCALE).then_inc(z_abs, 1)
                    act.wait_ge(z_abs, 4 * g + 4)
                    nc.scalar.activation(soft[:, :, :], soft[:, :, :], ACT.Exp, scale=-1.0).then_inc(z_exp, 1)
                    act.wait_ge(z_exp, g + 1)
                    nc.scalar.activation(soft[:, :, :], soft[:, :, :], ACT.Ln, bias=1.0).then_inc(z_log, 1)

                def weight_functions(g):
                    act.wait_ge(log_weights, 4 * g + 4)
                    nc.scalar.activation(z[:, :, :], z[:, :, :], ACT.Exp).then_inc(weights_exp, 1)

                def take_heads_high(g):
                    for h in range(CT):
                        act.wait_ge(heads_multiplied, 16 * g + 12 + h + 1)
                        nc.scalar.activation(gs[:, bass.ds(CT * g + h, 1), 0:T].rearrange("p o t -> p (o t)"),
                                             bank[4 + h][:, 0:T], ACT.Copy).then_inc(heads_high, 1)

                def copy_values(g):
                    for h in range(CT):
                        act.wait_ge(heads_multiplied, 16 * g + h + 1)
                        nc.scalar.activation(v_n[:, h, :], bank[4 + h][:, 0:T], ACT.Copy).then_inc(v_copied, 1)

                def qkv_group(g, first=False):
                    c = C0["qkv"] + 3 * DC * g
                    for k in range(3 * DC):
                        if not (first and k < 2):
                            take_high(c, k)
                        if k == 0 and not first:
                            cross_of(g - 1, 2)
                        if k == 2 and not first:
                            score_functions(g - 1)
                        if k == 4:
                            if not first:
                                weight_functions(g - 1)
                            cross_of(g, 0)
                        if k == 6 and not first:
                            take_heads_high(g - 1)
                        if k == 8:
                            copy_values(g)
                            cross_of(g, 1)

                qkv_group(0, first=True)
                with act.Fori(1, NG) as g:
                    qkv_group(g)

                def attn_out_group(dg):
                    c = C0["attn_out"] + DC * dg
                    for k in range(DC):
                        take_high(c, k)
                        if isinstance(dg, int) and dg == 0:
                            if k == 0:
                                cross_of(NG - 1, 2)
                            if k == 1:
                                score_functions(NG - 1)
                            if k == 2:
                                weight_functions(NG - 1)
                            if k == 3:
                                take_heads_high(NG - 1)
                        elif k == 0:
                            empty_residual(2, G0["attn_out"] + dg - 1, dg - 1, c - 1)
                        if isinstance(dg, int) and dg == 1 and k == 2:
                            copy_centre(2)

                attn_out_group(0)
                attn_out_group(1)
                with act.Fori(2, NG) as dg:
                    attn_out_group(dg)
                take_high(C0["up1"], 0)
                empty_residual(2, G0["attn_out"] + NG - 1, NG - 1, C0["up1"] - 1,
                               between=lambda: take_high(C0["up1"], 1, which=(0,)))
                finish_norm(2, after=lambda: take_high(C0["up1"], 1, which=(1,)))

        @block.vector
        def _(dve):
            steps = [0]

            def step(instruction):
                steps[0] += 1
                instruction.then_inc(vector_steps, 1)
                dve.wait_ge(vector_steps, steps[0])

            def take_low(c, k, rows=KT, tiles=CT, which=(0, 1)):
                for h in which:
                    cols = halves(tiles)[h]
                    dve.wait_ge(weights_high, 2 * c + h + 1)
                    nc.vector.tensor_tensor(low[k % 2][:, 0:rows, cols], raw[k % 4][:, 0:rows, cols],
                                            high[k % 2][:, 0:rows, cols].bitcast(f32),
                                            ALU.subtract).then_inc(weights_split, 1)

            def add_terms(G, ct, dst, tiles=CT, banks=0, scale=1.0):
                dve.wait_ge(cross_copied, 4 * G + ct + 1)
                if isinstance(scale, float):
                    op = nc.vector.tensor_tensor(dst, bank[banks + ct][:, 0:T], cross[:, ct % 2, :], ALU.add)
                else:
                    op = nc.vector.scalar_tensor_tensor(out=dst, in0=bank[banks + ct][:, 0:T], scalar=scale,
                                                        in1=cross[:, ct % 2, :], op0=ALU.mult, op1=ALU.add)
                op.then_inc(evacuated, steps_of(ct, tiles))

            def per_tile(t, n):
                return t.unsqueeze(1).broadcast_to([P, n, T])

            def prepare(L, dg):
                part = bass.ds(CT * dg, CT)
                x_low, x_hi = xs[:, part, T:2 * T].bitcast(f32), xs[:, part, 0:T].bitcast(f32)
                if isinstance(dg, int) and dg == 0:
                    op = nc.vector.tensor_scalar(r[:, part, :], x_low, ALPHA, None, ALU.mult)
                else:
                    dve.wait_ge(centre_copied, L + 1)
                    op = nc.vector.scalar_tensor_tensor(out=r[:, part, :], in0=x_low, scalar=ALPHA,
                                                        in1=per_tile(centre[:, :], CT),
                                                        op0=ALU.mult, op1=ALU.subtract)
                op.then_inc(half_prepared, 1)
                dve.wait_ge(half_prepared, NG * (L - 1) + dg + 1)
                nc.vector.scalar_tensor_tensor(out=r[:, part, :], in0=x_hi, scalar=ALPHA, in1=r[:, part, :],
                                               op0=ALU.mult, op1=ALU.add).then_inc(prepared, 1)

            def row(i):
                return r[:, bass.ds(i, 1), :].rearrange("p o t -> p (o t)")

            def empty_first(L, G, scaled=False, between=None):
                for ct in range(CT + 1):
                    if ct < CT:
                        if ct > 1:
                            dve.wait_ge(vector_steps, steps[0])
                        add_terms(G, ct, total[:, ct % 2, :], scale=pscale[:, ct:ct + 1] if scaled else 1.0)
                    if ct:
                        n = ct - 1
                        dve.wait_ge(evacuated, 4 * G + n + 1)
                        if L:
                            dve.wait_ge(prepared, NG * L + 1)
                            op = nc.vector.tensor_tensor(r[:, n, :], total[:, n % 2, :], r[:, n, :], ALU.add)
                        else:
                            dve.wait_ge(x_copied, n // 2 + 1)
                            op = nc.vector.scalar_tensor_tensor(out=r[:, n, :], in0=r[:, n, :], scalar=ALPHA,
                                                                in1=total[:, n % 2, :], op0=ALU.mult, op1=ALU.add)
                        op.then_inc(vector_steps, 1)
                        steps[0] += 1
                    if ct == 2 and between:
                        between()
                dve.wait_ge(vector_steps, steps[0])
                nc.vector.tensor_reduce(out=sum_c[:, :], in_=r[:, 0:CT, :].rearrange("p i t -> p t i"),
                                        axis=AX.X, op=ALU.add).then_inc(part_summed, 1)

            def centre_first(L):
                dve.wait_ge(centre_copied, L + 1)
                nc.vector.tensor_tensor(r[:, 0:CT, :], r[:, 0:CT, :], per_tile(centre[:, :], CT),
                                        ALU.subtract).then_inc(centred, CT)
                dve.wait_ge(centred, XT * L + CT)
                nc.vector.tensor_reduce(out=sum_c[:, :], in_=r[:, 0:CT, :].rearrange("p i t -> p t i"),
                                        axis=AX.X, op=ALU.add).then_inc(sums_c, CT)
                if L == 0:
                    return
                dve.wait_ge(squared, XT * L + 2)
                nc.vector.tensor_tensor(sum_q[:, :], squares[:, 0, :], squares[:, 1, :], ALU.add).then_inc(sums_q, 2)
                for i in (2, 3):
                    add_square(L, i, i)

            def add_centred(L, i):
                dve.wait_ge(sums_c, 12 * L + i)
                dve.wait_ge(centred, XT * L + i + 1)
                nc.vector.tensor_tensor(sum_c[:, :], sum_c[:, :], row(i), ALU.add).then_inc(sums_c, 1)

            def add_square(L, i, ct):
                dve.wait_ge(squared, XT * L + i + 1)
                dve.wait_ge(sums_q, 12 * L + i)
                nc.vector.tensor_tensor(sum_q[:, :], sum_q[:, :], squares[:, ct, :], ALU.add).then_inc(sums_q, 1)

            def empty_residual(L, G, dg, scaled=False, between=None):
                last = isinstance(dg, int) and dg == NG - 1
                summed_here = not last and not (isinstance(L, int) and L == 0)
                for ct in range(CT + 1):
                    i = CT * dg + ct
                    if ct < CT:
                        if ct > 1:
                            dve.wait_ge(centred, XT * L + i - 1)
                        add_terms(G, ct, total[:, ct % 2, :], scale=pscale[:, i:i + 1] if scaled else 1.0)
                    if ct:
                        n, i = ct - 1, i - 1
                        dve.wait_ge(evacuated, 4 * G + n + 1)
                        dve.wait_ge(prepared, NG * L + dg + 1)
                        nc.vector.tensor_tensor(row(i), total[:, n % 2, :], row(i), ALU.add).then_inc(centred, 1)
                        if summed_here:
                            add_centred(L, i)
                            if n:
                                add_square(L, i - 1, n - 1)
                    if ct == 2 and between:
                        between()
                if summed_here:
                    add_square(L, CT * dg + CT - 1, CT - 1)

            def finish_norm(L, last=False, after=None):
                scale = FIRST / D
                dve.wait_ge(stats_multiplied, 2 * L + 2)
                step(nc.vector.tensor_scalar(shift[:, :], bank[5][:, 0:T], scale, None, ALU.mult))
                step(nc.vector.tensor_tensor(rstd[:, :], shift[:, :], shift[:, :], ALU.mult))
                nc.vector.scalar_tensor_tensor(out=variance[:, :], in0=bank[6][:, 0:T], scalar=scale,
                                               in1=rstd[:, :], op0=ALU.mult,
                                               op1=ALU.subtract).then_inc(variance_ready, 1)
                step(nc.vector.tensor_tensor(r[:, 0:2, :], r[:, 0:2, :], per_tile(shift[:, :], 2), ALU.subtract))
                if after is not None:
                    after()
                dve.wait_ge(deviation_ready, L + 1)
                step(nc.vector.reciprocal(out=rstd[:, :], in_=deviation[:, :]))
                for b in range(XT // 2):
                    two = slice(2 * b, 2 * b + 2)
                    if b:
                        step(nc.vector.tensor_tensor(r[:, two, :], r[:, two, :], per_tile(shift[:, :], 2),
                                                     ALU.subtract))
                    nc.vector.tensor_tensor(r[:, two, :], r[:, two, :], per_tile(rstd[:, :], 2),
                                            ALU.mult).then_inc(normalized, 1)
                    if not last and b:
                        take_x_low(L, b - 1)
                if not last:
                    take_x_low(L, XT // 2 - 1)

            def take_x_low(L, b):
                two = slice(2 * b, 2 * b + 2)
                dve.wait_ge(x_high, 8 * L + b + 1)
                nc.vector.tensor_tensor(xs[:, two, T:2 * T], r[:, two, :], xs[:, two, 0:T].bitcast(f32),
                                        ALU.subtract).then_inc(x_split, 1)

            nc.vector.memset(count[:, 0:1], 1.0).then_inc(vector_steps, 1)
            for t in range(1, PAD):
                nc.vector.memset(count[:, t:t + 1], 1.0 / (t + 1)).then_inc(vector_steps, 1)
            steps[0] += PAD
            for g, w in enumerate(WINDOWS):
                nc.vector.memset(band[:, g, :, :], 1.0 / w).then_inc(band_filled, 1)
                nc.vector.memset(corner[:, g, :], 1.0 / w).then_inc(band_filled, 1)
                dve.wait_ge(vector_steps, steps[0])
                dve.wait_ge(band_filled, 3 * g + 1)
                nc.vector.tensor_copy(band[:, g, 0, 0:w - 1], count[:, 0:w - 1]).then_inc(band_filled, 1)
            dve.wait_ge(consts_ready, 2)
            for g in range(NG):
                dve.wait_ge(band_cut, 3 * g + 3)
                nc.vector.tensor_tensor(band[:, g, :, :], band[:, g, :, :],
                                        ident[:, :].unsqueeze(1).broadcast_to([P, 2, P]),
                                        ALU.subtract).then_inc(band_ready, 1)

            def pooled_low(g):
                for n in range(2):
                    two = slice(CT * g + 2 * n, CT * g + 2 * n + 2)
                    dve.wait_ge(pool_high, 2 * g + n + 1)
                    nc.vector.tensor_tensor(gs[:, two, T:2 * T],
                                            bank[4 + 2 * (g % 2) + n][:, :].rearrange("p (i t) -> p i t", i=2),
                                            gs[:, two, 0:T].bitcast(f32), ALU.subtract).then_inc(pool_split, 1)

            def prepare_input(g):
                part = slice(CT * g, CT * g + CT)
                dve.wait_ge(centre_copied, 1)
                dve.wait_ge(x_copied, 2 * g + 2)
                nc.vector.scalar_tensor_tensor(out=r[:, part, :], in0=r[:, part, :], scalar=ALPHA,
                                               in1=per_tile(centre[:, :], CT), op0=ALU.mult,
                                               op1=ALU.subtract).then_inc(prepared, 2 if g == 1 else 1)

            pooled_low(0)
            pooled_low(1)
            take_low(0, 0)
            pooled_low(2)
            take_low(1, 1)
            pooled_low(3)
            dve.wait_ge(params_copied, 2)
            empty_first(0, 0, scaled=True)
            take_low(2, 2)
            centre_first(0)
            prepare_input(1)
            empty_residual(0, 1, 1, scaled=True)
            take_low(3, 3)
            prepare_input(2)
            empty_residual(0, 2, 2, scaled=True)
            take_low(C0["up0"], 0)
            prepare_input(3)
            empty_residual(0, 3, 3, scaled=True, between=lambda: take_low(C0["up0"] + 1, 1, which=(0,)))
            finish_norm(0, after=lambda: take_low(C0["up0"] + 1, 1, which=(1,)))
            dve.wait_ge(params_copied, 4)

            def add_taps(layer, j, half, between):
                tiles = group_tiles(j)
                G = G0[f"up{layer}"] + 2 * j + half
                n = 2 * UJ * CT * layer + CT * (2 * j + half)
                target = value if half else gate

                def taps(ct):
                    col = half * FT + j * CT + ct
                    dve.wait_ge(first_tap, n + ct + 1)
                    nc.vector.scalar_tensor_tensor(out=convs[:, ct % 2, :], in0=hidden[:, ct % 2, 1:1 + T],
                                                   scalar=convp[:, 4 * layer + 1, bass.ds(col, 1)],
                                                   in1=convs[:, ct % 2, :], op0=ALU.mult, op1=ALU.add
                                                   ).then_inc(middle_tap, steps_of(ct, tiles))
                    dve.wait_ge(middle_tap, n + ct + 1)
                    nc.vector.scalar_tensor_tensor(out=target[:, ct, :], in0=hidden[:, ct % 2, 0:T],
                                                   scalar=convp[:, 4 * layer, bass.ds(col, 1)],
                                                   in1=convs[:, ct % 2, :], op0=ALU.mult, op1=ALU.add
                                                   ).then_inc(convolved, steps_of(ct, tiles))

                done = (2 * UJ + 1) * CT * layer + CT + CT * (2 * j + half)
                if half == 0 and not (isinstance(j, int) and UJ * layer + j == 0):
                    dve.wait_ge(inner_split, UJ * layer + j)
                for ct in range(tiles):
                    dve.wait_ge(convolved, done + ct - 1)
                    add_terms(G, ct, hidden[:, ct % 2, 2:2 + T], tiles, banks=4 * half)
                    if ct:
                        taps(ct - 1)
                    if ct == 2:
                        between()
                taps(tiles - 1)

            def multiply_gate(layer, j):
                tiles = group_tiles(j)
                dve.wait_ge(silu_done, UJ * layer + j + 1)
                dve.wait_ge(convolved, (2 * UJ + 1) * CT * layer + CT + CT * (2 * j + 2))
                nc.vector.tensor_tensor(value[:, 0:tiles, :], gate[:, 0:tiles, :], value[:, 0:tiles, :],
                                        ALU.mult).then_inc(products, 1)

            def take_inner_low(layer, j):
                tiles = group_tiles(j)
                part = bass.ds(j * CT, tiles)
                dve.wait_ge(inner_high, UJ * layer + j + 1)
                nc.vector.tensor_tensor(gs[:, part, T:2 * T], value[:, 0:tiles, :], gs[:, part, 0:T].bitcast(f32),
                                        ALU.subtract).then_inc(inner_split, 1)

            def up_group(layer, j, first=False):
                c0, tiles = C0[f"up{layer}"] + 2 * DC * j, group_tiles(j)
                for k in range(2 * DC):
                    if k in (1, 5):
                        if not (first and k == 1):
                            take_low(c0 + k, k, tiles=tiles, which=(1,))
                    elif not (first and k == 0):
                        take_low(c0 + k, k, tiles=tiles)
                    if not first:
                        if k == 0:
                            add_taps(layer, j - 1, 1, lambda: take_low(c0 + 1, 1, tiles=tiles, which=(0,)))
                        if k == 1:
                            multiply_gate(layer, j - 1)
                        if k == 2:
                            take_inner_low(layer, j - 1)
                    if k == 4:
                        add_taps(layer, j, 0, lambda: take_low(c0 + 5, 5, tiles=tiles, which=(0,)))

            for layer in range(DEPTH):
                dve.wait_ge(x_split, 16 * layer + 8)
                nc.vector.memset(hidden[:, :, 0:2], 0.0).then_inc(convolved, CT)
                dve.wait_ge(convolved, (2 * UJ + 1) * CT * layer + CT)
                up_group(layer, 0, first=True)
                with dve.Fori(1, UJ - 1) as j:
                    up_group(layer, j)
                up_group(layer, UJ - 1)
                c0, g0, L = C0[f"down{layer}"], G0[f"down{layer}"], 2 * layer + 1

                def down_group(dg):
                    def half_a():
                        take_low(c0 + FC * dg + 1, 1, DOWN_ROWS[1], which=(0,))

                    for k in range(FC):
                        take_low(c0 + FC * dg + k, k, DOWN_ROWS[k], which=(1,) if k == 1 else (0, 1))
                        if isinstance(dg, int) and dg == 0:
                            if k == 0:
                                add_taps(layer, UJ - 1, 1, half_a)
                            if k == 1:
                                multiply_gate(layer, UJ - 1)
                            if k == 2:
                                take_inner_low(layer, UJ - 1)
                            if k == 4:
                                dve.wait_ge(inner_split, UJ * layer + UJ)
                                prepare(L, 0)
                        elif isinstance(dg, int) and dg == 1:
                            if k == 0:
                                empty_first(L, g0, between=half_a)
                            if k == 2:
                                centre_first(L)
                            if k == 4:
                                prepare(L, 1)
                        else:
                            if k == 0:
                                empty_residual(L, g0 + dg - 1, dg - 1, between=half_a)
                            if k == 4:
                                prepare(L, dg)

                down_group(0)
                down_group(1)
                with dve.Fori(2, NG) as dg:
                    down_group(dg)
                if layer == 1:
                    empty_residual(L, g0 + NG - 1, NG - 1)
                    finish_norm(L, last=True)
                    break
                take_low(C0["qkv"], 0)
                empty_residual(L, g0 + NG - 1, NG - 1,
                               between=lambda: take_low(C0["qkv"] + 1, 1, which=(0,)))
                finish_norm(L, after=lambda: take_low(C0["qkv"] + 1, 1, which=(1,)))

                def heads_in(g, part):
                    target = (v_t, q_t, k_t)[part]
                    for ct in range(CT):
                        add_terms(G0["qkv"] + 3 * g + part, ct, target[:, ct, :])

                def score_functions(g):
                    dve.wait_ge(z_log, g + 1)
                    nc.vector.scalar_tensor_tensor(out=soft[:, :, :], in0=z[:, :, :], scalar=0.0,
                                                   in1=soft[:, :, :], op0=ALU.max, op1=ALU.add).then_inc(softplus, 1)

                def weight_logs(g):
                    for h in range(CT):
                        dve.wait_ge(heads_multiplied, 16 * g + 8 + h + 1)
                        nc.vector.scalar_tensor_tensor(out=z[:, h, :], in0=bank[4 + h][:, 0:3 * P],
                                                       scalar=-float(FIRST), in1=z[:, h, :],
                                                       op0=ALU.mult, op1=ALU.add).then_inc(log_weights, 1)

                def take_heads_low(g):
                    for h in range(CT):
                        i = bass.ds(CT * g + h, 1)
                        dve.wait_ge(heads_high, 4 * g + h + 1)
                        nc.vector.tensor_tensor(gs[:, i, T:2 * T].rearrange("p o t -> p (o t)"), bank[4 + h][:, 0:T],
                                                gs[:, i, 0:T].bitcast(f32).rearrange("p o t -> p (o t)"),
                                                ALU.subtract).then_inc(heads_split, 1)

                def qkv_group(g, first=False):
                    for k in range(3 * DC):
                        if not (first and k < 2):
                            take_low(C0["qkv"] + 3 * DC * g + k, k)
                        if k == 0 and not first:
                            heads_in(g - 1, 2)
                        if k == 2 and not first:
                            score_functions(g - 1)
                        if k == 4:
                            if not first:
                                weight_logs(g - 1)
                            heads_in(g, 0)
                        if k == 6 and not first:
                            take_heads_low(g - 1)
                        if k == 8:
                            heads_in(g, 1)

                qkv_group(0, first=True)
                with dve.Fori(1, NG) as g:
                    qkv_group(g)

                def attn_out_group(dg):
                    for k in range(DC):
                        take_low(C0["attn_out"] + DC * dg + k, k)
                        if isinstance(dg, int) and dg == 0:
                            if k == 0:
                                heads_in(NG - 1, 2)
                            if k == 1:
                                prepare(2, 0)
                                score_functions(NG - 1)
                            if k == 2:
                                weight_logs(NG - 1)
                            if k == 3:
                                take_heads_low(NG - 1)
                        elif isinstance(dg, int) and dg == 1:
                            if k == 0:
                                empty_first(2, G0["attn_out"])
                            if k == 2:
                                centre_first(2)
                                prepare(2, 1)
                        else:
                            if k == 0:
                                empty_residual(2, G0["attn_out"] + dg - 1, dg - 1)
                            if k == 2:
                                prepare(2, dg)

                attn_out_group(0)
                attn_out_group(1)
                with dve.Fori(2, NG) as dg:
                    attn_out_group(dg)
                take_low(C0["up1"], 0)
                empty_residual(2, G0["attn_out"] + NG - 1, NG - 1,
                               between=lambda: take_low(C0["up1"] + 1, 1, which=(0,)))
                finish_norm(2, after=lambda: take_low(C0["up1"] + 1, 1, which=(1,)))

            for n in range(2 * NG):
                dq, tt = n // 2, n % 2
                dve.wait_ge(out_transposed, n + 1)
                nc.vector.tensor_copy(o_sb[:, tt, dq * WC:(dq + 1) * WC], bank[n][:, :]).then_inc(out_copied, 1)

        @block.tensor
        def _(pe):
            def multiply(c, k, rhs, rows, tiles=CT, banks=0, first=False, last=False, before=None, between=None,
                         row_waits=None):
                def products(ct, kk):
                    w = (slice(None), kk, slice(ct * P, ct * P + P))
                    nc.tensor.matmul(bank[banks + ct][:, :], high[k % 2][w], rhs[kk],
                                     start=first and kk == 0, stop=False)
                    op = nc.tensor.matmul(bank[banks + ct][:, T:2 * T], low[k % 2][w], rhs[kk][:, 0:T],
                                          start=False, stop=last and kk == rows - 1)
                    if kk == rows - 1:
                        op.then_inc(tiles_multiplied, steps_of(ct, tiles))

                def tile_waits(ct):
                    if ct % 2 == 0:
                        pe.wait_ge(weights_split, 2 * c + ct // 2 + 1)
                    if before is not None:
                        pe.wait_ge(evacuated, 4 * before + ct + 1)

                if row_waits:
                    for kk in range(rows):
                        if kk % 2 == 0:
                            pe.wait_ge(x_split, row_waits[kk // 2])
                        for ct in range(tiles):
                            if kk == 0:
                                tile_waits(ct)
                            products(ct, kk)
                    return
                for ct in range(tiles):
                    tile_waits(ct)
                    for kk in range(rows):
                        products(ct, kk)
                    if ct == 1 and between:
                        between()

            def find_centre(L):
                pe.wait_ge(part_summed, L + 1)
                nc.tensor.matmul(bank[4][:, 0:T], mean_w[:, :], sum_c[:, :], start=True,
                                 stop=True).then_inc(centre_multiplied, 1)

            def statistics(L):
                pe.wait_ge(sums_c, 12 * L + 12)
                nc.tensor.matmul(bank[5][:, 0:T], mean_w[:, :], sum_c[:, :], start=True, stop=False)
                pe.wait_ge(sums_q, 12 * L + 12)
                nc.tensor.matmul(bank[6][:, 0:T], mean_w[:, :], sum_q[:, :], start=True, stop=False)
                for i in range(XT - CT, XT):
                    end = i == XT - 1
                    pe.wait_ge(centred, XT * L + i + 1)
                    one = nc.tensor.matmul(bank[5][:, 0:T], mean_w[:, :], r[:, i, :], start=False, stop=end)
                    if end:
                        one.then_inc(stats_multiplied, 1)
                    pe.wait_ge(squared, XT * L + i + 1)
                    two = nc.tensor.matmul(bank[6][:, 0:T], mean_w[:, :], squares[:, i % 4, :], start=False, stop=end)
                    if end:
                        two.then_inc(stats_multiplied, 1)

            pe.wait_ge(consts_ready, 2)

            def pool_tokens(g):
                pe.wait_ge(x_loaded[g], 16)
                pe.wait_ge(band_ready, g + 1)
                if g > 1:
                    pe.wait_ge(pool_split, 2 * g - 2)
                for n in range(CT):
                    i, b = CT * g + n, bank[4 + 2 * (g % 2) + n // 2]
                    now, nxt = x_in[:, 0, i * P:(i + 1) * P], x_in[:, 1, i * P:(i + 1) * P]
                    t0 = (n % 2) * T
                    nc.tensor.matmul(b[:, t0:t0 + P], now, band[:, g, 0, :], start=True, stop=False)
                    nc.tensor.matmul(b[:, t0 + P:t0 + T], nxt, band[:, g, 1, :], start=False, stop=False)
                    op = nc.tensor.matmul(b[:, t0 + P:t0 + P + PAD], now, corner[:, g, :], start=False, stop=True)
                    if n % 2:
                        op.then_inc(pool_multiplied, 1)

            def transpose_input(g):
                for i in range(CT * g, CT * g + CT):
                    for tt in range(TT):
                        at_col = (i % 2) * T + tt * P
                        op = nc.tensor.transpose(bank[i // 2][:, at_col:at_col + P],
                                                 x_in[:, tt, i * P:(i + 1) * P], ident[:, :])
                    if i % 2:
                        op.then_inc(x_transposed, 1)

            def transpose_taps(layer, b):
                for n in range(4):
                    op = nc.tensor.transpose(bank[b][:, n * 2 * FT:(n + 1) * 2 * FT],
                                             conv_in[:, 4 * layer + n, :], ident[0:2 * FT, 0:2 * FT])
                op.then_inc(params_transposed, 1)

            def pool_group(g):
                pe.wait_ge(pool_split, 2 * g + 2)
                multiply(g, g, [gs[:, CT * g + kk, :] for kk in range(KT)], KT, first=True, last=True,
                         before=g - 1 if g else None)

            pool_tokens(0)
            transpose_input(0)
            pe.wait_ge(params_loaded, 16 * 5)
            nc.tensor.transpose(bank[2][:, 0:XT], pscale_in[:, :], ident[0:XT, 0:XT]).then_inc(params_transposed, 1)
            nc.tensor.transpose(bank[3][:, 0:P], ln_in[:, :], ident[:, :]).then_inc(params_transposed, 1)
            pool_tokens(1)
            pe.wait_ge(params_copied, 2)
            transpose_input(1)
            pool_tokens(2)
            pe.wait_ge(x_copied, 4)
            pool_group(0)
            pool_tokens(3)
            pe.wait_ge(pool_split, 6)
            transpose_input(2)
            pool_group(1)
            pe.wait_ge(pool_split, 8)
            transpose_input(3)
            pe.wait_ge(x_copied, 6)
            pe.wait_ge(consts_ready, 6)
            find_centre(0)
            pe.wait_ge(conv_loaded, 16 * 4 * DEPTH)
            pe.wait_ge(x_copied, 8)
            transpose_taps(0, 7)
            pool_group(2)
            pe.wait_ge(centre_copied, 1)
            transpose_taps(1, 4)
            pool_group(3)
            statistics(0)

            for layer in range(DEPTH):
                def up_group(j):
                    tiles = group_tiles(j)
                    for half in range(2):
                        for k in range(DC):
                            G = G0[f"up{layer}"] + 2 * j + half
                            done = 16 * layer + 2 * k
                            if k:
                                pe.wait_ge(x_split, done + 2)
                            multiply(C0[f"up{layer}"] + 2 * DC * j + DC * half + k, k,
                                     [xs[:, k * KT + kk, :] for kk in range(KT)], KT, tiles, 4 * half,
                                     first=k == 0, last=k == DC - 1, before=G - 2 if k == 0 else None,
                                     row_waits=None if k or half else (done + 1, done + 2))

                with pe.Fori(0, UJ - 1) as j:
                    up_group(j)
                up_group(UJ - 1)

                c0, g0, L = C0[f"down{layer}"], G0[f"down{layer}"], 2 * layer + 1

                def down_group(dg):
                    for k in range(FC):
                        start, rows = sum(DOWN_ROWS[:k]), DOWN_ROWS[k]
                        pe.wait_ge(inner_split, UJ * layer + (start + rows - 1) // CT + 1)
                        before = (g0 - 2 if isinstance(dg, int) and dg == 0 else g0 + dg - 1) if k == 0 else None
                        multiply(c0 + FC * dg + k, k, [gs[:, start + kk, :] for kk in range(rows)], rows,
                                 first=k == 0, last=k == FC - 1, before=before)
                        if isinstance(dg, int) and dg == 1 and k == 0:
                            find_centre(L)

                down_group(0)
                down_group(1)
                with pe.Fori(2, NG) as dg:
                    down_group(dg)
                statistics(L)
                if layer == 1:
                    break

                def transpose_values(g):
                    if isinstance(g, int) and g == 0:
                        pe.wait_ge(evacuated, 4 * G0["qkv"] + 4)
                    else:
                        pe.wait_ge(evacuated, 4 * (G0["qkv"] + 3 * g) + 4)
                        pe.wait_ge(heads_split, 4 * g)
                    for h in range(CT):
                        for kt in range(TT):
                            op = nc.tensor.transpose(bank[4 + h][:, kt * P:(kt + 1) * P],
                                                     v_t[:, h, kt * P:(kt + 1) * P], ident[:, :])
                        op.then_inc(heads_multiplied, 1)

                def scores(g):
                    pe.wait_ge(evacuated, 4 * (G0["qkv"] + 3 * g + 2) + 4)
                    for h in range(CT):
                        pe.wait_ge(v_copied, 4 * g + h + 1)
                        nc.tensor.matmul(bank[4 + h][:, 0:T], k_t[:, h, 0:P], q_t[:, h, :], start=True, stop=False)
                        nc.tensor.matmul(bank[4 + h][:, T:T + P], k_t[:, h, P:T], q_t[:, h, P:T], start=False,
                                         stop=True).then_inc(heads_multiplied, 1)

                def sum_softplus(g):
                    pe.wait_ge(masked, 4 * g + 2)
                    for h in range(CT):
                        pe.wait_ge(z_copied, 4 * g + h + 1)
                        nc.tensor.matmul(bank[4 + h][:, 0:T], tri_w[:, :], soft[:, h, 0:T], start=True, stop=False)
                        nc.tensor.matmul(bank[4 + h][:, T:T + P], tri_w[:, :], soft[:, h, T:T + P], start=False,
                                         stop=False)
                        nc.tensor.matmul(bank[4 + h][:, P:T], mean_w[:, :], soft[:, h, T:T + P], start=False,
                                         stop=True).then_inc(heads_multiplied, 1)

                def weigh_values(g):
                    pe.wait_ge(masked, 4 * g + 4)
                    for h in range(CT):
                        nc.tensor.matmul(bank[4 + h][:, 0:T], v_n[:, h, 0:P], z[:, h, 0:T], start=True, stop=False)
                        nc.tensor.matmul(bank[4 + h][:, P:T], v_n[:, h, P:T], z[:, h, T:T + P], start=False,
                                         stop=True).then_inc(heads_multiplied, 1)

                def qkv_group(g, first=False):
                    for k in range(3 * DC):
                        part, n = k // DC, k % DC
                        start_rows = (9, 10) if first and k == 0 else None
                        if not start_rows:
                            pe.wait_ge(x_split, 8 + 2 * (n + 1))
                        G = G0["qkv"] + 3 * g + part
                        multiply(C0["qkv"] + 3 * DC * g + k, k, [xs[:, n * KT + kk, :] for kk in range(KT)], KT,
                                 first=n == 0, last=n == DC - 1, before=G - 1 if n == 0 else None,
                                 row_waits=start_rows)
                        if not first:
                            if k == 0:
                                scores(g - 1)
                            if k == 2:
                                sum_softplus(g - 1)
                            if k == 4:
                                weigh_values(g - 1)
                        if k == 6:
                            transpose_values(g)

                qkv_group(0, first=True)
                with pe.Fori(1, NG) as g:
                    qkv_group(g)

                def attn_out_group(dg):
                    for k in range(DC):
                        pe.wait_ge(heads_split, 4 * k + 4)
                        G = G0["attn_out"] + dg
                        multiply(C0["attn_out"] + DC * dg + k, k, [gs[:, k * KT + kk, :] for kk in range(KT)], KT,
                                 first=k == 0, last=k == DC - 1, before=G - 1 if k == 0 else None,
                                 between=(lambda: scores(NG - 1)) if isinstance(dg, int) and dg + k == 0 else None)
                        if isinstance(dg, int) and dg == 0:
                            if k == 1:
                                sum_softplus(NG - 1)
                            if k == 2:
                                weigh_values(NG - 1)
                        if isinstance(dg, int) and dg == 1 and k == 0:
                            find_centre(2)

                attn_out_group(0)
                attn_out_group(1)
                with pe.Fori(2, NG) as dg:
                    attn_out_group(dg)
                statistics(2)

            for n in range(2 * NG):
                dq, tt = n // 2, n % 2
                pe.wait_ge(affine, XT * 3 + CT * dq + CT)
                if n == 0:
                    pe.wait_ge(evacuated, 4 * G0["end"])
                if n == 5:
                    pe.wait_ge(variance_ready, 4)
                for q in range(CT):
                    op = nc.tensor.transpose(bank[n][:, q * P:(q + 1) * P],
                                             r[:, CT * dq + q, tt * P:(tt + 1) * P], ident[:, :])
                op.then_inc(out_transposed, 1)


INPUTS = ["x", "pool_w", "pool_scale", "attn_w_qkv", "attn_w_o", "ffn_w_up", "ffn_conv_w", "ffn_conv_b",
          "ffn_w_down", "ln_mix_g", "ln_mix_b", "ln_ffn_g", "ln_ffn_b"]


def kernel(**inputs):
    import numpy as np
    import concourse.bacc as bacc
    from concourse.bass_utils import run_bass_kernel_spmd

    nc = bacc.Bacc("TRN2", target_bir_lowering=False, num_devices=1, dynamic_dma_scratch_size=4096)
    arrays, args = {}, []
    for name in INPUTS:
        a = np.ascontiguousarray(inputs[name])
        arrays[f"in_{name}"] = a
        args.append(nc.dram_tensor(f"in_{name}", a.shape, mybir.dt.from_np(a.dtype), kind="ExternalInput").ap())
    shape = inputs["x"].shape
    out = nc.dram_tensor("out_x", shape, mybir.dt.float32, kind="ExternalOutput").ap()
    decoder_trunk(nc, *args, out)
    result = run_bass_kernel_spmd(nc, [arrays], core_ids=[0])
    return result.results[0]["out_x"]
```

```python
import concourse.bass as bass
from concourse import mybir
from contextlib import ExitStack


def decoder_trunk(nc, x, pool_w, pool_scale, attn_w_qkv, attn_w_o, ffn_w_up, ffn_conv_w, ffn_conv_b,
                  ffn_w_down, ln_mix_g, ln_mix_b, ln_ffn_g, ln_ffn_b, out):
    f32 = mybir.dt.float32
    f32r = mybir.dt.float32r
    ALU = mybir.AluOpType
    ACT = mybir.ActivationFunctionType
    AX = mybir.AxisListType

    P = 128
    T = x.shape[1]
    D = x.shape[2]
    DEPTH = ffn_w_up.shape[0]
    FF = ffn_w_down.shape[1]
    TT = T // P
    XT = D // P
    FT = FF // P
    CT = 4
    KT = 4
    WC = CT * P
    NG = XT // CT
    TAPS = ffn_conv_w.shape[1]
    ALPHA = float((2.0 * DEPTH) ** 0.25)
    EPS = 1e-5
    ZSCALE = float(P) ** -0.5
    WINDOWS = (2, 4, 8, 16)
    PAD = WINDOWS[-1]
    FIRST = CT * P
    SUMMED = XT - 2
    SCALAR_PIECES = (3, 2 * NG - 1)
    VECTOR_PIECES = tuple(n for n in range(2 * NG) if n not in SCALAR_PIECES)
    FIRST_SUMMED = 10
    assert (T, TT, XT, NG, TAPS, DEPTH) == (2 * P, 2, 16, 4, 3, 2) and FF == FT * P

    UJ = -(-FT // CT)
    LAST_TILES = FT - (UJ - 1) * CT
    D_ROWS = [KT] * (XT // KT)
    DOWN_ROWS = [3, 3, 3, 2] + [4] * 8
    assert sum(DOWN_ROWS) == FT and len(DOWN_ROWS) % 4 == 0
    DC, FC = len(D_ROWS), len(DOWN_ROWS)

    names = ["pool", "up0", "down0", "qkv", "attn_out", "up1", "down1", "end"]
    chunks = [NG, 2 * UJ * DC, NG * FC, 3 * NG * DC, NG * DC, 2 * UJ * DC, NG * FC]
    groups = [NG, 2 * UJ, NG, 3 * NG, NG, 2 * UJ, NG]
    C0 = {n: sum(chunks[:i]) for i, n in enumerate(names)}
    G0 = {n: sum(groups[:i]) for i, n in enumerate(names)}
    assert all(c % 4 == 0 for c in C0.values())

    ctx = ExitStack()
    with ctx:
        top = [-(-nc.sbuf_base // 64) * 64]

        def at(name, shape, dtype, offset):
            return nc.alloc_sbuf_tensor_at(name, shape, dtype, offset=offset)

        def place(name, shape, dtype):
            size = 4
            for n in shape[1:]:
                size *= n
            t = at(name, shape, dtype, top[0])
            top[0] += -(-size // 64) * 64
            return t

        raw = [place(f"raw{i}", [P, KT, WC], f32) for i in range(4)]
        high = [place(f"weights_high{i}", [P, KT, WC], f32r) for i in range(2)]
        low = [place(f"weights_low{i}", [P, KT, WC], f32r) for i in range(2)]
        xs_at = top[0]
        xs = place("xs", [P, XT, 2 * T], f32r)
        r_at = top[0]
        r = place("r", [P, XT, T], f32)
        gs_at = top[0]
        gs = place("gs", [P, FT, 2 * T], f32r)
        cross = place("cross", [P, 2, T], f32)
        total = place("total", [P, 2, T], f32)
        centre = place("centre", [P, T], f32)
        sum_c = place("sum_c", [P, T], f32)
        sum_q = place("sum_q", [P, T], f32)
        squares = place("squares", [P, 4, T], f32)
        shift = place("shift", [P, T], f32)
        variance = place("variance", [P, T], f32)
        deviation = place("deviation", [P, T], f32)
        rstd = place("rstd", [P, T], f32)
        ident = place("ident", [P, P], f32)
        mean_w = place("mean_w", [P, P], f32)
        tri_w = place("tri_w", [P, P], f32)
        convp = place("convp", [P, 4 * DEPTH, 2 * FT], f32)
        lnp = place("lnp", [P, 4, DEPTH, XT], f32)
        pscale = place("pscale", [P, XT], f32)
        count = place("count", [P, PAD], f32)
        eps = place("eps", [P, 1], f32)
        assert top[0] <= nc.sbuf_usable_end

        hidden = at("hidden", [P, 2, T + 2], f32, r_at)
        convs = at("convs", [P, 2, T], f32, r_at + 2112)
        gate = at("gate", [P, CT, T], f32, r_at + 4160)
        value = at("value", [P, CT, T], f32, r_at + 8256)
        free = gs_at + XT * 2 * T * 4
        x_in = at("x_in", [P, TT, D], f32, free)
        band = at("band", [P, NG, 2, P], f32, free + 16384)
        corner = at("corner", [P, NG, PAD], f32, free + 20480)
        conv_in = at("conv_in", [2 * FT, 4 * DEPTH, P], f32, free + 46592)
        ln_in = at("ln_in", [P, P], f32, free + 50688)
        pscale_in = at("pscale_in", [XT, P], f32, free + 51200)
        first_squares = at("first_squares", [P, XT, T], f32, xs_at)
        q_t = at("q_t", [P, CT, T], f32, free + 4096)
        k_t = at("k_t", [P, CT, T], f32, free + 8192)
        v_n = at("v_n", [P, TT, WC], f32, free + 12288)
        z = at("z", [P, CT, 3 * P], f32, free + 16384)
        soft = at("soft", [P, CT, 3 * P], f32, free + 22528)
        soft_high = at("soft_high", [P, CT, 3 * P], f32r, free + 28672)
        soft_low = at("soft_low", [P, CT, 3 * P], f32r, free + 34816)
        tri_r = at("tri_r", [P, P], f32r, free + 40960)
        mean_r = at("mean_r", [P, P], f32r, free + 41472)
        o_sb = at("o_sb", [P, TT, D], f32, gs_at)

        bank = [ctx.enter_context(nc.psum_tensor(f"bank{i}", [P, WC], f32)) for i in range(8)]

        def sem(name):
            return ctx.enter_context(nc.semaphore(name))

        weights_loaded = [sem(f"weights_loaded{i}") for i in range(4)]
        weights_high = sem("weights_high_ready")
        weights_split = sem("weights_split")
        tiles_multiplied = sem("tiles_multiplied")
        cross_copied = sem("cross_copied")
        evacuated = sem("evacuated")
        x_loaded = [sem(f"x_loaded{g}") for g in range(NG)]
        pscale_loaded, params_loaded = sem("pscale_loaded"), sem("params_loaded")
        consts_ready = sem("consts_ready")
        band_filled, band_cut, band_ready = sem("band_filled"), sem("band_cut"), sem("band_ready")
        x_transposed, x_copied = sem("x_transposed"), sem("x_copied")
        params_transposed, params_copied = sem("params_transposed"), sem("params_copied")
        pool_multiplied, pool_high, pool_split = (
            sem("pool_multiplied"), sem("pool_high"), sem("pool_split"))
        part_summed = sem("part_summed")
        centre_multiplied, centre_copied = sem("centre_multiplied"), sem("centre_copied")
        half_prepared, prepared = sem("half_prepared"), sem("prepared")
        late_prepared = sem("late_prepared")
        centred = sem("centred")
        squared = sem("squared")
        sums_c, sums_q = sem("sums_c"), sem("sums_q")
        first_sums_c, first_sums_q = sem("first_sums_c"), sem("first_sums_q")
        stats_multiplied = sem("stats_multiplied")
        variance_ready, deviation_ready = sem("variance_ready"), sem("deviation_ready")
        shift_ready = sem("shift_ready")
        shifted = sem("shifted")
        normalized = sem("normalized")
        affine = sem("affine")
        x_high, x_split = sem("x_high"), sem("x_split")
        first_tap, middle_tap, convolved = sem("first_tap"), sem("middle_tap"), sem("convolved")
        silu_done, products, inner_high, inner_split = (
            sem("silu_done"), sem("products"), sem("inner_high"), sem("inner_split"))
        heads_multiplied = sem("heads_multiplied")
        z_copied = sem("z_copied")
        z_abs, z_exp, z_log, softplus = sem("z_abs"), sem("z_exp"), sem("z_log"), sem("softplus")
        masked = sem("masked")
        soft_taken, soft_split = sem("soft_taken"), sem("soft_split")
        sum_weights_ready = sem("sum_weights_ready")
        log_weights, weights_exp = sem("log_weights"), sem("weights_exp")
        heads_high, heads_split = sem("heads_high"), sem("heads_split")
        out_transposed, out_copied, out_stored = sem("out_transposed"), sem("out_copied"), sem("out_stored")
        out_copied_scalar = sem("out_copied_scalar")
        vector_steps = sem("vector_steps")

        block = ctx.enter_context(nc.Block())

        def halves(tiles):
            return (slice(0, 2 * P), slice(2 * P, tiles * P))

        def group_tiles(j):
            return LAST_TILES if isinstance(j, int) and j == UJ - 1 else CT

        def steps_of(ct, tiles):
            return CT - ct if ct == tiles - 1 else 1

        @block.sync
        def _(sp):

            def load(c0, k, matrix, row_tile, rows, col, tiles=CT):
                c = c0 + k
                if not (isinstance(c, int) and c < 4):
                    sp.wait_ge(weights_split, 2 * (c - 4) + 2)
                source = matrix[row_tile * P:(row_tile + rows) * P, bass.ds(col, tiles * P)]
                sp.dma_start(raw[k % 4][:, 0:rows, 0:tiles * P],
                             source.rearrange("(t p) n -> p t n", p=P)).then_inc(weights_loaded[k % 4], 16)

            def load_up(layer, c0, j):
                for k in range(2 * DC):
                    half = k // DC
                    load(c0 + 2 * DC * j, k, ffn_w_up[layer], (k % DC) * KT, KT,
                         half * FF + j * WC, group_tiles(j))

            def load_down(layer, c0):
                with sp.Fori(0, NG) as dg:
                    for k in range(FC):
                        load(c0 + FC * dg, k, ffn_w_down[layer], sum(DOWN_ROWS[:k]), DOWN_ROWS[k], dg * WC)

            for g in range(NG):
                sp.dma_start(x_in[:, :, g * WC:(g + 1) * WC],
                             x[0, :, g * WC:(g + 1) * WC].rearrange("(t p) d -> p t d", p=P)
                             ).then_inc(x_loaded[g], 16)
                load(0, g, pool_w[0, g], 0, KT, 0)
            for n, source in enumerate((ln_mix_g, ln_mix_b, ln_ffn_g, ln_ffn_b)):
                sp.dma_start(ln_in[n * DEPTH * XT:(n + 1) * DEPTH * XT, :],
                             source.rearrange("l (t p) -> (l t) p", p=P)).then_inc(params_loaded, 16)
            for layer in range(DEPTH):
                sp.dma_start(conv_in[:, 4 * layer:4 * layer + TAPS, :],
                             ffn_conv_w[layer].rearrange("i (t p) -> t i p", p=P)).then_inc(params_loaded, 16)
                sp.dma_start(conv_in[:, 4 * layer + TAPS, :],
                             ffn_conv_b[layer].rearrange("(t p) -> t p", p=P)).then_inc(params_loaded, 16)
            for layer in range(DEPTH):
                up = C0[f"up{layer}"]
                with sp.Fori(0, UJ - 1) as j:
                    load_up(layer, up, j)
                load_up(layer, up, UJ - 1)
                load_down(layer, C0[f"down{layer}"])
                if layer == 0:
                    qkv = attn_w_qkv[0].rearrange("k (s n) -> s k n", s=3)
                    with sp.Fori(1, NG + 1) as g:
                        for n, part in enumerate((0, 1, 2)):
                            for k in range(DC):
                                load(C0["qkv"] + 3 * DC * g - 3 * DC, n * DC + k, qkv[part], k * KT, KT,
                                     g * WC - WC)
                    with sp.Fori(0, NG) as dg:
                        for k in range(DC):
                            load(C0["attn_out"] + DC * dg, k, attn_w_o[0], k * KT, KT, dg * WC)
            for n in range(2 * NG):
                dq, tt = n // 2, n % 2
                if n in SCALAR_PIECES:
                    sp.wait_ge(out_copied_scalar, SCALAR_PIECES.index(n) + 1)
                else:
                    sp.wait_ge(out_copied, VECTOR_PIECES.index(n) + 1)
                sp.dma_start(out[0, tt * P:(tt + 1) * P, dq * WC:(dq + 1) * WC],
                             o_sb[:, tt, dq * WC:(dq + 1) * WC]).then_inc(out_stored, 16)
            sp.wait_ge(out_stored, 16 * 2 * NG)

        @block.gpsimd
        def _(pool):
            nc.gpsimd.memset(ident[:, :], 0.0).then_inc(consts_ready, 1)
            pool.wait_ge(consts_ready, 1)
            nc.gpsimd.affine_select(out=ident[:, :], in_=ident[:, :], compare_op=ALU.not_equal, fill=1.0,
                                    base=0, pattern=[[-1, P]], channel_multiplier=1).then_inc(consts_ready, 1)
            for g, w in enumerate(WINDOWS):
                pool.wait_ge(band_filled, 3 * g + 3)
                both = band[:, g, :, :]
                nc.gpsimd.affine_select(out=both, in_=both, compare_op=ALU.is_ge, fill=0.0, base=0,
                                        pattern=[[0, 2], [1, P]], channel_multiplier=-1).then_inc(band_cut, 1)
                pool.wait_ge(band_cut, 3 * g + 1)
                nc.gpsimd.affine_select(out=both, in_=both, compare_op=ALU.is_ge, fill=0.0, base=w - 1,
                                        pattern=[[0, 2], [-1, P]], channel_multiplier=1).then_inc(band_cut, 1)
                nc.gpsimd.affine_select(out=corner[:, g, :], in_=corner[:, g, :], compare_op=ALU.is_ge, fill=0.0,
                                        base=w - 1 - P, pattern=[[-1, PAD]],
                                        channel_multiplier=1).then_inc(band_cut, 1)
            nc.gpsimd.memset(mean_w[:, :], 1.0 / FIRST).then_inc(consts_ready, 1)
            nc.gpsimd.memset(tri_w[:, :], 1.0 / FIRST).then_inc(consts_ready, 1)
            nc.gpsimd.memset(eps[:, :], EPS).then_inc(consts_ready, 1)
            pool.wait_ge(consts_ready, 5)
            nc.gpsimd.affine_select(out=tri_w[:, :], in_=tri_w[:, :], compare_op=ALU.is_ge, fill=0.0,
                                    base=0, pattern=[[-1, P]], channel_multiplier=1).then_inc(consts_ready, 1)

            pool.wait_ge(centre_copied, 1)
            for g in (2, 3):
                part = slice(CT * g, CT * g + CT)
                pool.wait_ge(x_copied, 2 * g + 2)
                nc.gpsimd.tensor_tensor(r[:, part, :], r[:, part, :],
                                        centre[:, :].unsqueeze(1).broadcast_to([P, CT, T]),
                                        ALU.subtract).then_inc(late_prepared, 1)

            pool.wait_ge(centre_multiplied, 1)
            for i in range(1, FIRST_SUMMED):
                pool.wait_ge(centred, i + 1)
                if i > 1:
                    pool.wait_ge(first_sums_c, i - 1)
                nc.gpsimd.tensor_tensor(sum_c[:, :], r[:, 0, :] if i == 1 else sum_c[:, :], r[:, i, :],
                                        ALU.add).then_inc(first_sums_c, 1)
                pool.wait_ge(squared, i + 1)
                if i > 1:
                    pool.wait_ge(first_sums_q, i - 1)
                nc.gpsimd.tensor_tensor(sum_q[:, :], first_squares[:, 0, :] if i == 1 else sum_q[:, :],
                                        first_squares[:, i, :], ALU.add).then_inc(first_sums_q, 1)

            def subtract_shift(L):
                pool.wait_ge(shift_ready, L + 1)
                for b in range(1, XT // 2 if L < 3 else XT // 2 - 2):
                    two = slice(2 * b, 2 * b + 2)
                    nc.gpsimd.tensor_tensor(r[:, two, :], r[:, two, :],
                                            shift[:, :].unsqueeze(1).broadcast_to([P, 2, T]),
                                            ALU.subtract).then_inc(shifted, 1)

            subtract_shift(0)
            subtract_shift(1)

            def mask(tile, block_at):
                part = tile[:, :, block_at * P:(block_at + 1) * P]
                nc.gpsimd.affine_select(out=part, in_=part, compare_op=ALU.is_gt, fill=0.0, base=0,
                                        pattern=[[0, CT], [1, P]], channel_multiplier=-1).then_inc(masked, 1)

            for g in range(NG):
                pool.wait_ge(softplus, g + 1)
                mask(soft, 0)
                mask(soft, 2)
                pool.wait_ge(weights_exp, g + 1)
                mask(z, 0)
                mask(z, 2)
            subtract_shift(2)
            subtract_shift(3)

        @block.scalar
        def _(act):
            act.dma_start(pscale_in[:, :], pool_scale[0].rearrange("(t p) -> t p", p=P)).then_inc(pscale_loaded, 16)

            def take_high(c0, k, rows=KT, tiles=CT, which=(0, 1)):
                c = c0 + k
                if 0 in which:
                    act.wait_ge(weights_loaded[k % 4], 4 * c0 + 16 * (k // 4 + 1))
                for h in which:
                    cols = halves(tiles)[h]
                    if not (isinstance(c, int) and c < 2):
                        act.wait_ge(tiles_multiplied, 4 * (c - 2) + 2 * h + 2)
                    nc.scalar.activation(high[k % 2][:, 0:rows, cols], raw[k % 4][:, 0:rows, cols],
                                         ACT.Copy).then_inc(weights_high, 1)

            def copy_cross(G, c_end, ct, tiles=CT, banks=0, scale=None):
                act.wait_ge(tiles_multiplied, 4 * c_end + ct + 1)
                if not (isinstance(G, int) and G == 0 and ct < 2):
                    act.wait_ge(evacuated, 4 * G + ct - 1)
                source = bank[banks + ct][:, T:2 * T]
                if scale is None:
                    op = nc.scalar.activation(cross[:, ct % 2, :], source, ACT.Copy)
                else:
                    op = nc.scalar.activation(cross[:, ct % 2, :], source, ACT.Identity, scale=scale)
                op.then_inc(cross_copied, steps_of(ct, tiles))

            def squares_of(L, dg, ct):
                i = CT * dg + ct
                act.wait_ge(centred, XT * L + i + 1)
                if L and not (isinstance(dg, int) and dg == 0):
                    act.wait_ge(sums_q, SUMMED * (L - 1) + i - 3)
                nc.scalar.activation(squares[:, ct, :] if L else first_squares[:, i, :], r[:, bass.ds(i, 1), :].rearrange("p o t -> p (o t)"),
                                     ACT.Square).then_inc(squared, 1)

            def empty_residual(L, G, dg, c_end, scaled=False, between=None):
                for ct in range(CT):
                    i = CT * dg + ct
                    copy_cross(G, c_end, ct, scale=pscale[:, i:i + 1] if scaled else None)
                    if ct and not (isinstance(dg, int) and dg == 0):
                        squares_of(L, dg, ct - 1)
                    if ct == 2 and between:
                        between()
                if not (isinstance(dg, int) and dg == 0):
                    squares_of(L, dg, CT - 1)

            def copy_centre(L, between=None):
                act.wait_ge(centre_multiplied, L + 1)
                nc.scalar.activation(centre[:, :], bank[4][:, 0:T], ACT.Copy).then_inc(centre_copied, 1)
                if between:
                    between()
                for ct in range(CT):
                    squares_of(L, 0, ct)

            def finish_norm(L, next_chunks=None):
                which, layer = (0 if L % 2 == 0 else 2), L // 2
                act.wait_ge(variance_ready, L + 1)
                nc.scalar.activation(deviation[:, :], variance[:, :], ACT.Sqrt, bias=eps[:, :]).then_inc(deviation_ready, 1)
                if next_chunks is not None:
                    take_high(next_chunks, 1)

                def copy_output(n):
                    act.wait_ge(out_transposed, n + 1)
                    nc.scalar.activation(o_sb[:, n % 2, n // 2 * WC:(n // 2 + 1) * WC], bank[n][:, :],
                                         ACT.Copy).then_inc(out_copied_scalar, 1)

                for start, n in [(0, 1), (1, 1)] + [(i, 2) for i in range(2, XT, 2)]:
                    act.wait_ge(normalized, XT * L + start + n)
                    for i in range(start, start + n):
                        nc.scalar.activation(r[:, i, :], r[:, i, :], ACT.Identity,
                                             scale=lnp[:, which, layer, i:i + 1],
                                             bias=lnp[:, which + 1, layer, i:i + 1]).then_inc(affine, 1)
                    if next_chunks is not None:
                        act.wait_ge(affine, XT * L + start + n)
                        nc.scalar.activation(xs[:, start:start + n, 0:T], r[:, start:start + n, :],
                                             ACT.Copy).then_inc(x_high, n)
                        if start == 8:
                            take_high(next_chunks, 2)
                        if start == 12:
                            take_high(next_chunks, 3)
                    elif start == 12:
                        copy_output(SCALAR_PIECES[0])
                if next_chunks is None:
                    copy_output(SCALAR_PIECES[1])

            def pairs(b):
                return bank[b][:, :].rearrange("p (i t) -> p i t", i=2)

            def pooled_high(g):
                for n in range(2):
                    act.wait_ge(pool_multiplied, 2 * g + n + 1)
                    nc.scalar.activation(gs[:, CT * g + 2 * n:CT * g + 2 * n + 2, 0:T],
                                         pairs(4 + 2 * (g % 2) + n), ACT.Copy).then_inc(pool_high, 1)

            def copy_input(g):
                for n in (2 * g, 2 * g + 1):
                    two = slice(2 * n, 2 * n + 2)
                    act.wait_ge(x_transposed, n + 1)
                    nc.scalar.activation(r[:, two, :], pairs(n), ACT.Copy, scale=ALPHA).then_inc(x_copied, 1)

            def copy_taps(layer, b):
                act.wait_ge(params_transposed, 2 + layer)
                nc.scalar.activation(convp[:, 4 * layer:4 * layer + 4, :],
                                     bank[b][:, 0:4 * 2 * FT].rearrange("p (n t) -> p n t", n=4),
                                     ACT.Copy).then_inc(params_copied, 1)

            act.wait_ge(params_transposed, 1)
            nc.scalar.activation(pscale[:, :], bank[6][:, 0:XT], ACT.Copy).then_inc(params_copied, 1)
            pooled_high(0)
            take_high(0, 0)
            copy_input(0)
            pooled_high(1)
            copy_input(1)
            take_high(0, 1)
            pooled_high(2)
            act.wait_ge(params_copied, 1)
            empty_residual(0, 0, 0, 0, scaled=True)
            pooled_high(3)
            copy_input(2)
            take_high(0, 2)
            copy_input(3)
            copy_centre(0, between=lambda: take_high(0, 3, which=(0,)))
            empty_residual(0, 1, 1, 1, scaled=True, between=lambda: take_high(0, 3, which=(1,)))
            copy_taps(0, 7)
            nc.scalar.activation(lnp[:, :, :, :], bank[7][:, 8 * FT:8 * FT + P].rearrange(
                "p (n l t) -> p n l t", n=4, l=DEPTH), ACT.Copy).then_inc(params_copied, 1)
            empty_residual(0, 2, 2, 2, scaled=True, between=lambda: take_high(C0["up0"], 0, which=(0,)))
            take_high(C0["up0"], 0, which=(1,))
            copy_taps(1, 4)
            act.wait_ge(params_copied, 4)
            empty_residual(0, 3, 3, 3, scaled=True)
            finish_norm(0, C0["up0"])

            def up_cross(layer, j, half, between):
                tiles = group_tiles(j)
                G = G0[f"up{layer}"] + 2 * j + half
                c_end = C0[f"up{layer}"] + 2 * DC * j + DC * (half + 1) - 1
                n = (2 * UJ + 1) * CT * layer + CT + CT * (2 * j + half)

                def tap(ct):
                    col = half * FT + j * CT + ct
                    act.wait_ge(evacuated, 4 * G + ct + 1)
                    act.wait_ge(convolved, n + ct - 1)
                    nc.scalar.activation(convs[:, ct % 2, :], hidden[:, ct % 2, 2:2 + T], ACT.Identity,
                                         scale=convp[:, 4 * layer + 2, bass.ds(col, 1)],
                                         bias=convp[:, 4 * layer + 3, bass.ds(col, 1)]
                                         ).then_inc(first_tap, steps_of(ct, tiles))

                for ct in range(tiles):
                    copy_cross(G, c_end, ct, tiles, banks=4 * half)
                    if ct:
                        tap(ct - 1)
                    if ct == 2:
                        between()
                tap(tiles - 1)

            def apply_silu(layer, j):
                tiles = group_tiles(j)
                act.wait_ge(convolved, (2 * UJ + 1) * CT * layer + CT + CT * (2 * j + 1))
                nc.scalar.activation(gate[:, 0:tiles, :], gate[:, 0:tiles, :], ACT.Silu).then_inc(silu_done, 1)

            def take_inner_high(layer, j):
                tiles = group_tiles(j)
                act.wait_ge(products, UJ * layer + j + 1)
                nc.scalar.activation(gs[:, bass.ds(j * CT, tiles), 0:T], value[:, 0:tiles, :],
                                     ACT.Copy).then_inc(inner_high, 1)

            def up_group(layer, j, first=False):
                c0, tiles = C0[f"up{layer}"] + 2 * DC * j, group_tiles(j)
                for k in range(2 * DC):
                    if not (first and k < 4):
                        take_high(c0, k, tiles=tiles, which=(1,) if k in (1, 5) else (0, 1))
                    if k == 0 and not first:
                        up_cross(layer, j - 1, 1, lambda: take_high(c0, 1, tiles=tiles, which=(0,)))
                    if k == 2 and not first:
                        take_inner_high(layer, j - 1)
                    if k == 4:
                        up_cross(layer, j, 0, lambda: take_high(c0, 5, tiles=tiles, which=(0,)))
                    if k == 5:
                        apply_silu(layer, j)

            for layer in range(DEPTH):
                up_group(layer, 0, first=True)
                with act.Fori(1, UJ - 1) as j:
                    up_group(layer, j)
                up_group(layer, UJ - 1)
                c0, g0, L = C0[f"down{layer}"], G0[f"down{layer}"], 2 * layer + 1

                def down_group(dg):
                    def half_a():
                        take_high(c0 + FC * dg, 1, DOWN_ROWS[1], which=(0,))

                    for k in range(FC):
                        take_high(c0 + FC * dg, k, DOWN_ROWS[k], which=(1,) if k == 1 else (0, 1))
                        if isinstance(dg, int) and dg == 0:
                            if k == 0:
                                up_cross(layer, UJ - 1, 1, half_a)
                            if k == 2:
                                take_inner_high(layer, UJ - 1)
                        elif k == 0:
                            empty_residual(L, g0 + dg - 1, dg - 1, c0 + FC * dg - 1, between=half_a)
                        if isinstance(dg, int) and dg == 1 and k == 2:
                            copy_centre(L)

                down_group(0)
                down_group(1)
                with act.Fori(2, NG) as dg:
                    down_group(dg)
                if layer == 1:
                    empty_residual(L, g0 + NG - 1, NG - 1, c0 + FC * NG - 1)
                    finish_norm(L)
                    break
                take_high(C0["qkv"], 0)
                empty_residual(L, g0 + NG - 1, NG - 1, c0 + FC * NG - 1)
                finish_norm(L, C0["qkv"])

                def copy_values(g):
                    c_end = C0["qkv"] + 3 * DC * g + 3 * DC - 1
                    act.wait_ge(tiles_multiplied, 4 * c_end + 3)
                    nc.scalar.activation(v_n[:, 0, :], bank[4][:, :], ACT.Copy).then_inc(cross_copied, CT)

                def cross_of(g, part):
                    for ct in range(CT):
                        copy_cross(G0["qkv"] + 3 * g + part, C0["qkv"] + 3 * DC * g + DC * (part + 1) - 1, ct)

                def score_functions(g):
                    for h in range(CT):
                        act.wait_ge(heads_multiplied, 12 * g + h + 1)
                        nc.scalar.activation(z[:, h, :], bank[4 + h][:, 0:3 * P], ACT.Copy,
                                             scale=ZSCALE).then_inc(z_copied, 1)
                        nc.scalar.activation(soft[:, h, :], bank[4 + h][:, 0:3 * P], ACT.Abs,
                                             scale=ZSCALE).then_inc(z_abs, 1)
                    act.wait_ge(z_abs, 4 * g + 4)
                    nc.scalar.activation(soft[:, :, :], soft[:, :, :], ACT.Exp, scale=-1.0).then_inc(z_exp, 1)
                    act.wait_ge(z_exp, g + 1)
                    nc.scalar.activation(soft[:, :, :], soft[:, :, :], ACT.Ln, bias=1.0).then_inc(z_log, 1)

                def take_soft_high(g):
                    act.wait_ge(masked, 4 * g + 2)
                    nc.scalar.activation(soft_high[:, :, :], soft[:, :, :], ACT.Copy).then_inc(soft_taken, 1)

                def weight_functions(g):
                    act.wait_ge(log_weights, 4 * g + 4)
                    nc.scalar.activation(z[:, :, :], z[:, :, :], ACT.Exp).then_inc(weights_exp, 1)

                def take_heads_high(g):
                    for h in range(CT):
                        act.wait_ge(heads_multiplied, 12 * g + 8 + h + 1)
                        nc.scalar.activation(gs[:, bass.ds(CT * g + h, 1), 0:T].rearrange("p o t -> p (o t)"),
                                             bank[4 + h][:, 0:T], ACT.Copy).then_inc(heads_high, 1)

                def qkv_group(g, first=False):
                    c = C0["qkv"] + 3 * DC * g
                    for k in range(3 * DC):
                        if not (first and k < 4):
                            take_high(c, k)
                        if k == 4:
                            cross_of(g, 0)
                        if k == 8:
                            cross_of(g, 1)
                        if first:
                            continue
                        if k == 0:
                            copy_values(g - 1)
                        if k == 2:
                            score_functions(g - 1)
                        if k == 3:
                            take_soft_high(g - 1)
                        if k == 5:
                            weight_functions(g - 1)
                        if k == 7:
                            take_heads_high(g - 1)

                qkv_group(0, first=True)
                with act.Fori(1, NG) as g:
                    qkv_group(g)

                def attn_out_group(dg):
                    c = C0["attn_out"] + DC * dg
                    for k in range(DC):
                        take_high(c, k)
                        if isinstance(dg, int) and dg == 0:
                            if k == 0:
                                copy_values(NG - 1)
                            if k == 1:
                                score_functions(NG - 1)
                            if k == 2:
                                weight_functions(NG - 1)
                            if k == 3:
                                take_heads_high(NG - 1)
                        elif k == 0:
                            empty_residual(2, G0["attn_out"] + dg - 1, dg - 1, c - 1)
                        if isinstance(dg, int) and dg == 1 and k == 2:
                            copy_centre(2)

                attn_out_group(0)
                attn_out_group(1)
                with act.Fori(2, NG) as dg:
                    attn_out_group(dg)
                take_high(C0["up1"], 0)
                empty_residual(2, G0["attn_out"] + NG - 1, NG - 1, C0["up1"] - 1)
                finish_norm(2, C0["up1"])

        @block.vector
        def _(dve):
            steps = [0]

            def step(instruction):
                steps[0] += 1
                instruction.then_inc(vector_steps, 1)
                dve.wait_ge(vector_steps, steps[0])

            def take_low(c, k, rows=KT, tiles=CT, which=(0, 1)):
                for h in which:
                    cols = halves(tiles)[h]
                    dve.wait_ge(weights_high, 2 * c + h + 1)
                    nc.vector.tensor_tensor(low[k % 2][:, 0:rows, cols], raw[k % 4][:, 0:rows, cols],
                                            high[k % 2][:, 0:rows, cols].bitcast(f32),
                                            ALU.subtract).then_inc(weights_split, 1)

            def add_terms(G, ct, dst, tiles=CT, banks=0, scale=1.0):
                dve.wait_ge(cross_copied, 4 * G + ct + 1)
                if isinstance(scale, float):
                    op = nc.vector.tensor_tensor(dst, bank[banks + ct][:, 0:T], cross[:, ct % 2, :], ALU.add)
                else:
                    op = nc.vector.scalar_tensor_tensor(out=dst, in0=bank[banks + ct][:, 0:T], scalar=scale,
                                                        in1=cross[:, ct % 2, :], op0=ALU.mult, op1=ALU.add)
                op.then_inc(evacuated, steps_of(ct, tiles))

            def per_tile(t, n):
                return t.unsqueeze(1).broadcast_to([P, n, T])

            def prepare(L, dg):
                part = bass.ds(CT * dg, CT)
                x_low, x_hi = xs[:, part, T:2 * T].bitcast(f32), xs[:, part, 0:T].bitcast(f32)
                if isinstance(dg, int) and dg == 0:
                    op = nc.vector.tensor_scalar(r[:, part, :], x_low, ALPHA, None, ALU.mult)
                else:
                    dve.wait_ge(centre_copied, L + 1)
                    op = nc.vector.scalar_tensor_tensor(out=r[:, part, :], in0=x_low, scalar=ALPHA,
                                                        in1=per_tile(centre[:, :], CT),
                                                        op0=ALU.mult, op1=ALU.subtract)
                op.then_inc(half_prepared, 1)
                dve.wait_ge(half_prepared, NG * (L - 1) + dg + 1)
                nc.vector.scalar_tensor_tensor(out=r[:, part, :], in0=x_hi, scalar=ALPHA, in1=r[:, part, :],
                                               op0=ALU.mult, op1=ALU.add).then_inc(prepared, 1)

            def row(i):
                return r[:, bass.ds(i, 1), :].rearrange("p o t -> p (o t)")

            def empty_first(L, G, scaled=False, between=None):
                for ct in range(CT + 1):
                    if ct < CT:
                        if ct > 1:
                            dve.wait_ge(vector_steps, steps[0])
                        add_terms(G, ct, total[:, ct % 2, :], scale=pscale[:, ct:ct + 1] if scaled else 1.0)
                    if ct:
                        n = ct - 1
                        dve.wait_ge(evacuated, 4 * G + n + 1)
                        if L:
                            dve.wait_ge(prepared, NG * L + 1)
                        else:
                            dve.wait_ge(x_copied, n // 2 + 1)
                        nc.vector.tensor_tensor(r[:, n, :], total[:, n % 2, :], r[:, n, :],
                                                ALU.add).then_inc(vector_steps, 1)
                        steps[0] += 1
                    if ct == 2 and between:
                        between()
                dve.wait_ge(vector_steps, steps[0])
                nc.vector.tensor_reduce(out=sum_c[:, :], in_=r[:, 0:CT, :].rearrange("p i t -> p t i"),
                                        axis=AX.X, op=ALU.add).then_inc(part_summed, 1)

            def centre_first(L):
                dve.wait_ge(centre_copied, L + 1)
                nc.vector.tensor_tensor(r[:, 0:CT, :], r[:, 0:CT, :], per_tile(centre[:, :], CT),
                                        ALU.subtract).then_inc(centred, CT)
                if L == 0:
                    return
                dve.wait_ge(centred, XT * L + CT)
                nc.vector.tensor_reduce(out=sum_c[:, :], in_=r[:, 0:CT, :].rearrange("p i t -> p t i"),
                                        axis=AX.X, op=ALU.add).then_inc(sums_c, CT)
                dve.wait_ge(squared, XT * L + 2)
                nc.vector.tensor_tensor(sum_q[:, :], squares[:, 0, :], squares[:, 1, :], ALU.add).then_inc(sums_q, 2)
                for i in (2, 3):
                    add_square(L, i, i)

            def add_centred(L, i):
                dve.wait_ge(sums_c, SUMMED * (L - 1) + i)
                dve.wait_ge(centred, XT * L + i + 1)
                nc.vector.tensor_tensor(sum_c[:, :], sum_c[:, :], row(i), ALU.add).then_inc(sums_c, 1)

            def add_square(L, i, ct):
                dve.wait_ge(squared, XT * L + i + 1)
                dve.wait_ge(sums_q, SUMMED * (L - 1) + i)
                nc.vector.tensor_tensor(sum_q[:, :], sum_q[:, :], squares[:, ct, :], ALU.add).then_inc(sums_q, 1)

            def empty_residual(L, G, dg, scaled=False, between=None):
                last = isinstance(dg, int) and dg == NG - 1
                here = 0 if isinstance(L, int) and L == 0 else CT - (XT - SUMMED) if last else CT
                for ct in range(CT):
                    i = CT * dg + ct
                    if ct > 1:
                        dve.wait_ge(centred, XT * L + i - 1)
                    add_terms(G, ct, total[:, ct % 2, :], scale=pscale[:, i:i + 1] if scaled else 1.0)
                    if 0 < ct <= here:
                        add_centred(L, i - 1)
                    dve.wait_ge(evacuated, 4 * G + ct + 1)
                    if isinstance(L, int) and L == 0 and dg >= 2:
                        dve.wait_ge(late_prepared, dg - 1)
                    else:
                        dve.wait_ge(prepared, NG * L + dg + 1)
                    nc.vector.tensor_tensor(row(i), total[:, ct % 2, :], row(i), ALU.add).then_inc(centred, 1)
                    if 0 < ct <= here:
                        add_square(L, i - 1, ct - 1)
                    if ct == 2 and between:
                        between()
                if here == CT:
                    add_centred(L, CT * dg + CT - 1)
                    add_square(L, CT * dg + CT - 1, CT - 1)

            def finish_norm(L, next_chunks=None):
                scale = FIRST / D
                dve.wait_ge(stats_multiplied, 2 * L + 2)
                nc.vector.tensor_scalar(shift[:, :], bank[5][:, 0:T], scale, None, ALU.mult).then_inc(shift_ready, 1)
                dve.wait_ge(shift_ready, L + 1)
                step(nc.vector.tensor_tensor(rstd[:, :], shift[:, :], shift[:, :], ALU.mult))
                nc.vector.scalar_tensor_tensor(out=variance[:, :], in0=bank[6][:, 0:T], scalar=scale,
                                               in1=rstd[:, :], op0=ALU.mult,
                                               op1=ALU.subtract).then_inc(variance_ready, 1)
                step(nc.vector.tensor_tensor(r[:, 0:2, :], r[:, 0:2, :], per_tile(shift[:, :], 2), ALU.subtract))
                dve.wait_ge(deviation_ready, L + 1)
                step(nc.vector.reciprocal(out=rstd[:, :], in_=deviation[:, :]))
                for i in range(2):
                    nc.vector.tensor_tensor(row(i), row(i), rstd[:, :], ALU.mult).then_inc(normalized, 1)
                for b in range(1, XT // 2):
                    two = slice(2 * b, 2 * b + 2)
                    if L == 3 and b >= XT // 2 - 2:
                        step(nc.vector.tensor_tensor(r[:, two, :], r[:, two, :], per_tile(shift[:, :], 2),
                                                     ALU.subtract))
                    else:
                        dve.wait_ge(shifted, (XT // 2 - 1) * L + b)
                    nc.vector.tensor_tensor(r[:, two, :], r[:, two, :], per_tile(rstd[:, :], 2),
                                            ALU.mult).then_inc(normalized, 2)
                    if next_chunks is not None:
                        if b == 1:
                            take_x_low(L, 0, 1)
                            take_x_low(L, 1, 1)
                            take_low(next_chunks + 1, 1, which=(0,))
                        else:
                            take_x_low(L, 2 * b - 2, 2)
                        if b == 2:
                            take_low(next_chunks + 1, 1, which=(1,))
                        if b == 5:
                            take_low(next_chunks + 2, 2)
                        if b == 7:
                            take_low(next_chunks + 3, 3)
                    elif b in (5, 6):
                        copy_output(b - 5)
                    elif b == 7:
                        copy_output(2)
                if next_chunks is not None:
                    take_x_low(L, XT - 2, 2)
                else:
                    for n in VECTOR_PIECES[3:]:
                        copy_output(n)

            def copy_output(n):
                dve.wait_ge(out_transposed, n + 1)
                nc.vector.tensor_copy(o_sb[:, n % 2, n // 2 * WC:(n // 2 + 1) * WC],
                                      bank[n][:, :]).then_inc(out_copied, 1)

            def take_x_low(L, i, n):
                part = slice(i, i + n)
                dve.wait_ge(x_high, XT * L + i + n)
                nc.vector.tensor_tensor(xs[:, part, T:2 * T], r[:, part, :], xs[:, part, 0:T].bitcast(f32),
                                        ALU.subtract).then_inc(x_split, n)

            nc.vector.memset(count[:, 0:1], 1.0).then_inc(vector_steps, 1)
            for t in range(1, PAD):
                nc.vector.memset(count[:, t:t + 1], 1.0 / (t + 1)).then_inc(vector_steps, 1)
            steps[0] += PAD
            for g, w in enumerate(WINDOWS):
                nc.vector.memset(band[:, g, :, :], 1.0 / w).then_inc(band_filled, 1)
                nc.vector.memset(corner[:, g, :], 1.0 / w).then_inc(band_filled, 1)
                dve.wait_ge(vector_steps, steps[0])
                dve.wait_ge(band_filled, 3 * g + 1)
                nc.vector.tensor_copy(band[:, g, 0, 0:w - 1], count[:, 0:w - 1]).then_inc(band_filled, 1)
            dve.wait_ge(consts_ready, 2)
            for g in range(NG):
                dve.wait_ge(band_cut, 3 * g + 3)
                nc.vector.tensor_tensor(band[:, g, :, :], band[:, g, :, :],
                                        ident[:, :].unsqueeze(1).broadcast_to([P, 2, P]),
                                        ALU.subtract).then_inc(band_ready, 1)

            def pooled_low(g):
                for n in range(2):
                    two = slice(CT * g + 2 * n, CT * g + 2 * n + 2)
                    dve.wait_ge(pool_high, 2 * g + n + 1)
                    nc.vector.tensor_tensor(gs[:, two, T:2 * T],
                                            bank[4 + 2 * (g % 2) + n][:, :].rearrange("p (i t) -> p i t", i=2),
                                            gs[:, two, 0:T].bitcast(f32), ALU.subtract).then_inc(pool_split, 1)

            pooled_low(0)
            take_low(0, 0)
            pooled_low(1)
            take_low(1, 1)
            pooled_low(2)
            dve.wait_ge(params_copied, 1)
            empty_first(0, 0, scaled=True)
            pooled_low(3)
            take_low(2, 2)
            centre_first(0)
            take_low(3, 3, which=(0,))
            dve.wait_ge(x_copied, 4)
            nc.vector.tensor_tensor(r[:, CT:2 * CT, :], r[:, CT:2 * CT, :], per_tile(centre[:, :], CT),
                                    ALU.subtract).then_inc(prepared, NG)
            empty_residual(0, 1, 1, scaled=True, between=lambda: take_low(3, 3, which=(1,)))
            empty_residual(0, 2, 2, scaled=True, between=lambda: take_low(C0["up0"], 0, which=(0,)))
            take_low(C0["up0"], 0, which=(1,))
            empty_residual(0, 3, 3, scaled=True)
            finish_norm(0, C0["up0"])
            dve.wait_ge(params_copied, 4)

            def add_taps(layer, j, half, between):
                tiles = group_tiles(j)
                G = G0[f"up{layer}"] + 2 * j + half
                n = 2 * UJ * CT * layer + CT * (2 * j + half)
                target = value if half else gate

                def taps(ct):
                    col = half * FT + j * CT + ct
                    dve.wait_ge(first_tap, n + ct + 1)
                    nc.vector.scalar_tensor_tensor(out=convs[:, ct % 2, :], in0=hidden[:, ct % 2, 1:1 + T],
                                                   scalar=convp[:, 4 * layer + 1, bass.ds(col, 1)],
                                                   in1=convs[:, ct % 2, :], op0=ALU.mult, op1=ALU.add
                                                   ).then_inc(middle_tap, steps_of(ct, tiles))
                    dve.wait_ge(middle_tap, n + ct + 1)
                    nc.vector.scalar_tensor_tensor(out=target[:, ct, :], in0=hidden[:, ct % 2, 0:T],
                                                   scalar=convp[:, 4 * layer, bass.ds(col, 1)],
                                                   in1=convs[:, ct % 2, :], op0=ALU.mult, op1=ALU.add
                                                   ).then_inc(convolved, steps_of(ct, tiles))

                done = (2 * UJ + 1) * CT * layer + CT + CT * (2 * j + half)
                if half == 0 and not (isinstance(j, int) and UJ * layer + j == 0):
                    dve.wait_ge(inner_split, UJ * layer + j)
                for ct in range(tiles):
                    dve.wait_ge(convolved, done + ct - 1)
                    add_terms(G, ct, hidden[:, ct % 2, 2:2 + T], tiles, banks=4 * half)
                    if ct:
                        taps(ct - 1)
                    if ct == 2:
                        between()
                taps(tiles - 1)

            def multiply_gate(layer, j):
                tiles = group_tiles(j)
                dve.wait_ge(silu_done, UJ * layer + j + 1)
                dve.wait_ge(convolved, (2 * UJ + 1) * CT * layer + CT + CT * (2 * j + 2))
                nc.vector.tensor_tensor(value[:, 0:tiles, :], gate[:, 0:tiles, :], value[:, 0:tiles, :],
                                        ALU.mult).then_inc(products, 1)

            def take_inner_low(layer, j):
                tiles = group_tiles(j)
                part = bass.ds(j * CT, tiles)
                dve.wait_ge(inner_high, UJ * layer + j + 1)
                nc.vector.tensor_tensor(gs[:, part, T:2 * T], value[:, 0:tiles, :], gs[:, part, 0:T].bitcast(f32),
                                        ALU.subtract).then_inc(inner_split, 1)

            def up_group(layer, j, first=False):
                c0, tiles = C0[f"up{layer}"] + 2 * DC * j, group_tiles(j)
                for k in range(2 * DC):
                    if not (first and k < 4):
                        take_low(c0 + k, k, tiles=tiles, which=(1,) if k in (1, 5) else (0, 1))
                    if not first:
                        if k == 0:
                            add_taps(layer, j - 1, 1, lambda: take_low(c0 + 1, 1, tiles=tiles, which=(0,)))
                        if k == 1:
                            multiply_gate(layer, j - 1)
                        if k == 2:
                            take_inner_low(layer, j - 1)
                    if k == 4:
                        add_taps(layer, j, 0, lambda: take_low(c0 + 5, 5, tiles=tiles, which=(0,)))

            for layer in range(DEPTH):
                dve.wait_ge(x_split, 2 * XT * layer + XT)
                nc.vector.memset(hidden[:, :, 0:2], 0.0).then_inc(convolved, CT)
                dve.wait_ge(convolved, (2 * UJ + 1) * CT * layer + CT)
                up_group(layer, 0, first=True)
                with dve.Fori(1, UJ - 1) as j:
                    up_group(layer, j)
                up_group(layer, UJ - 1)
                c0, g0, L = C0[f"down{layer}"], G0[f"down{layer}"], 2 * layer + 1

                def down_group(dg):
                    def half_a():
                        take_low(c0 + FC * dg + 1, 1, DOWN_ROWS[1], which=(0,))

                    for k in range(FC):
                        take_low(c0 + FC * dg + k, k, DOWN_ROWS[k], which=(1,) if k == 1 else (0, 1))
                        if isinstance(dg, int) and dg == 0:
                            if k == 0:
                                add_taps(layer, UJ - 1, 1, half_a)
                            if k == 1:
                                multiply_gate(layer, UJ - 1)
                            if k == 2:
                                take_inner_low(layer, UJ - 1)
                            if k == 4:
                                dve.wait_ge(inner_split, UJ * layer + UJ)
                                prepare(L, 0)
                        elif isinstance(dg, int) and dg == 1:
                            if k == 0:
                                empty_first(L, g0, between=half_a)
                            if k == 2:
                                centre_first(L)
                            if k == 4:
                                prepare(L, 1)
                        else:
                            if k == 0:
                                empty_residual(L, g0 + dg - 1, dg - 1, between=half_a)
                            if k == 4:
                                prepare(L, dg)

                down_group(0)
                down_group(1)
                with dve.Fori(2, NG) as dg:
                    down_group(dg)
                if layer == 1:
                    empty_residual(L, g0 + NG - 1, NG - 1)
                    finish_norm(L)
                    break
                take_low(C0["qkv"], 0)
                empty_residual(L, g0 + NG - 1, NG - 1)
                finish_norm(L, C0["qkv"])

                def copy_values(g):
                    G, c_end = G0["qkv"] + 3 * g + 2, C0["qkv"] + 3 * DC * g + 3 * DC - 1
                    dve.wait_ge(tiles_multiplied, 4 * c_end + 4)
                    dve.wait_ge(cross_copied, 4 * G + CT)
                    nc.vector.tensor_copy(v_n[:, 1, :], bank[5][:, :]).then_inc(evacuated, CT)

                def heads_in(g, part):
                    target = (q_t, k_t)[part]
                    for ct in range(CT):
                        add_terms(G0["qkv"] + 3 * g + part, ct, target[:, ct, :])

                def score_functions(g):
                    dve.wait_ge(z_log, g + 1)
                    nc.vector.scalar_tensor_tensor(out=soft[:, :, :], in0=z[:, :, :], scalar=0.0,
                                                   in1=soft[:, :, :], op0=ALU.max, op1=ALU.add).then_inc(softplus, 1)

                def take_soft_low(g):
                    dve.wait_ge(soft_taken, g + 1)
                    nc.vector.tensor_tensor(soft_low[:, :, :], soft[:, :, :], soft_high[:, :, :].bitcast(f32),
                                            ALU.subtract).then_inc(soft_split, 1)

                def weight_logs(g):
                    for h in range(CT):
                        dve.wait_ge(heads_multiplied, 12 * g + 4 + h + 1)
                        nc.vector.scalar_tensor_tensor(out=z[:, h, :], in0=bank[4 + h][:, 0:3 * P],
                                                       scalar=-float(FIRST), in1=z[:, h, :],
                                                       op0=ALU.mult, op1=ALU.add).then_inc(log_weights, 1)

                def take_heads_low(g):
                    for h in range(CT):
                        i = bass.ds(CT * g + h, 1)
                        dve.wait_ge(heads_high, 4 * g + h + 1)
                        nc.vector.tensor_tensor(gs[:, i, T:2 * T].rearrange("p o t -> p (o t)"), bank[4 + h][:, 0:T],
                                                gs[:, i, 0:T].bitcast(f32).rearrange("p o t -> p (o t)"),
                                                ALU.subtract).then_inc(heads_split, 1)

                def qkv_group(g, first=False):
                    for k in range(3 * DC):
                        if not (first and k < 4):
                            take_low(C0["qkv"] + 3 * DC * g + k, k)
                        if k == 4:
                            heads_in(g, 0)
                        if k == 8:
                            heads_in(g, 1)
                        if first:
                            continue
                        if k == 0:
                            copy_values(g - 1)
                        if k == 2:
                            score_functions(g - 1)
                        if k == 3:
                            take_soft_low(g - 1)
                        if k == 5:
                            weight_logs(g - 1)
                        if k == 7:
                            take_heads_low(g - 1)

                nc.vector.tensor_copy(tri_r[:, :], tri_w[:, :]).then_inc(sum_weights_ready, 1)
                nc.vector.tensor_copy(mean_r[:, :], mean_w[:, :]).then_inc(sum_weights_ready, 1)
                qkv_group(0, first=True)
                with dve.Fori(1, NG) as g:
                    qkv_group(g)

                def attn_out_group(dg):
                    for k in range(DC):
                        take_low(C0["attn_out"] + DC * dg + k, k)
                        if isinstance(dg, int) and dg == 0:
                            if k == 0:
                                copy_values(NG - 1)
                            if k == 1:
                                prepare(2, 0)
                                score_functions(NG - 1)
                            if k == 2:
                                weight_logs(NG - 1)
                            if k == 3:
                                take_heads_low(NG - 1)
                        elif isinstance(dg, int) and dg == 1:
                            if k == 0:
                                empty_first(2, G0["attn_out"])
                            if k == 2:
                                centre_first(2)
                                prepare(2, 1)
                        else:
                            if k == 0:
                                empty_residual(2, G0["attn_out"] + dg - 1, dg - 1)
                            if k == 2:
                                prepare(2, dg)

                attn_out_group(0)
                attn_out_group(1)
                with dve.Fori(2, NG) as dg:
                    attn_out_group(dg)
                take_low(C0["up1"], 0)
                empty_residual(2, G0["attn_out"] + NG - 1, NG - 1)
                finish_norm(2, C0["up1"])

        @block.tensor
        def _(pe):
            def multiply(c, k, rhs, rows, tiles=CT, banks=0, first=False, last=False, before=None, between=None,
                         row_waits=None):
                def products(ct, kk):
                    w = (slice(None), kk, slice(ct * P, ct * P + P))
                    nc.tensor.matmul(bank[banks + ct][:, :], high[k % 2][w], rhs[kk],
                                     start=first and kk == 0, stop=False)
                    op = nc.tensor.matmul(bank[banks + ct][:, T:2 * T], low[k % 2][w], rhs[kk][:, 0:T],
                                          start=False, stop=last and kk == rows - 1)
                    if kk == rows - 1:
                        op.then_inc(tiles_multiplied, steps_of(ct, tiles))

                def tile_waits(ct):
                    if ct % 2 == 0:
                        pe.wait_ge(weights_split, 2 * c + ct // 2 + 1)
                    if before is not None:
                        pe.wait_ge(evacuated, 4 * before + ct + 1)

                if row_waits:
                    for kk in range(rows):
                        if not kk or row_waits[kk] > row_waits[kk - 1]:
                            pe.wait_ge(x_split, row_waits[kk])
                        for ct in range(tiles):
                            if kk == 0:
                                tile_waits(ct)
                            products(ct, kk)
                    return
                for ct in range(tiles):
                    tile_waits(ct)
                    for kk in range(rows):
                        products(ct, kk)
                    if between and ct in between:
                        between[ct]()

            def find_centre(L):
                pe.wait_ge(part_summed, L + 1)
                nc.tensor.matmul(bank[4][:, 0:T], mean_w[:, :], sum_c[:, :], start=True,
                                 stop=True).then_inc(centre_multiplied, 1)

            def keep_clock_up(n):
                for _ in range(n):
                    nc.tensor.matmul(bank[7][:, 0:P], ident[:, :], ident[:, :], start=True, stop=True)

            def sum_statistics(L):
                if L:
                    pe.wait_ge(sums_c, SUMMED * L)
                else:
                    pe.wait_ge(first_sums_c, FIRST_SUMMED - 1)
                nc.tensor.matmul(bank[5][:, 0:T], mean_w[:, :], sum_c[:, :], start=L > 0, stop=False)
                if L:
                    pe.wait_ge(sums_q, SUMMED * L)
                else:
                    pe.wait_ge(first_sums_q, FIRST_SUMMED - 1)
                nc.tensor.matmul(bank[6][:, 0:T], mean_w[:, :], sum_q[:, :], start=L > 0, stop=False)

            def tile_statistics(L, i):
                end = i == XT - 1
                pe.wait_ge(centred, XT * L + i + 1)
                one = nc.tensor.matmul(bank[5][:, 0:T], mean_w[:, :], r[:, i, :], start=not L and i == FIRST_SUMMED, stop=end)
                if end:
                    one.then_inc(stats_multiplied, 1)
                pe.wait_ge(squared, XT * L + i + 1)
                two = nc.tensor.matmul(bank[6][:, 0:T], mean_w[:, :], squares[:, i % 4, :] if L else first_squares[:, i, :],
                                       start=not L and i == FIRST_SUMMED, stop=end)
                if end:
                    two.then_inc(stats_multiplied, 1)

            def finish_statistics(L):
                sum_statistics(L)
                for i in range(SUMMED, XT):
                    tile_statistics(L, i)
                if L < 3:
                    keep_clock_up(24)

            pe.wait_ge(consts_ready, 2)
            keep_clock_up(7)
            pe.wait_ge(pscale_loaded, 16)
            nc.tensor.transpose(bank[6][:, 0:XT], pscale_in[:, :], ident[0:XT, 0:XT]).then_inc(params_transposed, 1)

            def pool_tokens(g):
                pe.wait_ge(x_loaded[g], 16)
                pe.wait_ge(band_ready, g + 1)
                if g > 1:
                    pe.wait_ge(pool_split, 2 * g - 2)
                for n in range(CT):
                    i, b = CT * g + n, bank[4 + 2 * (g % 2) + n // 2]
                    now, nxt = x_in[:, 0, i * P:(i + 1) * P], x_in[:, 1, i * P:(i + 1) * P]
                    t0 = (n % 2) * T
                    nc.tensor.matmul(b[:, t0:t0 + P], now, band[:, g, 0, :], start=True, stop=False)
                    nc.tensor.matmul(b[:, t0 + P:t0 + T], nxt, band[:, g, 1, :], start=False, stop=False)
                    op = nc.tensor.matmul(b[:, t0 + P:t0 + P + PAD], now, corner[:, g, :], start=False, stop=True)
                    if n % 2:
                        op.then_inc(pool_multiplied, 1)

            def transpose_input(g):
                for i in range(CT * g, CT * g + CT):
                    for tt in range(TT):
                        at_col = (i % 2) * T + tt * P
                        op = nc.tensor.transpose(bank[i // 2][:, at_col:at_col + P],
                                                 x_in[:, tt, i * P:(i + 1) * P], ident[:, :])
                    if i % 2:
                        op.then_inc(x_transposed, 1)

            def transpose_taps(layer, b):
                for n in range(4):
                    op = nc.tensor.transpose(bank[b][:, n * 2 * FT:(n + 1) * 2 * FT],
                                             conv_in[:, 4 * layer + n, :], ident[0:2 * FT, 0:2 * FT])
                if layer == 0:
                    op = nc.tensor.transpose(bank[b][:, 8 * FT:8 * FT + P], ln_in[:, :], ident[:, :])
                op.then_inc(params_transposed, 1)

            def pool_group(g, between=None):
                pe.wait_ge(pool_split, 2 * g + 2)
                multiply(g, g, [gs[:, CT * g + kk, :] for kk in range(KT)], KT, first=True, last=True,
                         before=g - 1 if g else None, between=between)

            def find_first_centre():
                pe.wait_ge(consts_ready, 6)
                pe.wait_ge(x_copied, 6)
                find_centre(0)

            pool_tokens(0)
            transpose_input(0)
            pe.wait_ge(params_copied, 1)
            pool_tokens(1)
            transpose_input(1)
            pool_tokens(2)
            pe.wait_ge(x_copied, 4)
            pool_group(0)
            pool_tokens(3)
            pe.wait_ge(pool_split, 6)
            transpose_input(2)
            pe.wait_ge(pool_split, 8)
            transpose_input(3)
            pool_group(1, between={1: find_first_centre})
            pe.wait_ge(params_loaded, 16 * (4 + 2 * DEPTH))
            pe.wait_ge(x_copied, 8)
            transpose_taps(0, 7)
            pool_group(2)
            pe.wait_ge(centre_copied, 1)
            transpose_taps(1, 4)
            pool_group(3)
            for i in range(FIRST_SUMMED, SUMMED):
                tile_statistics(0, i)
            finish_statistics(0)

            for layer in range(DEPTH):
                def up_group(j, behind_norm=False):
                    tiles = group_tiles(j)
                    for half in range(2):
                        for k in range(DC):
                            G = G0[f"up{layer}"] + 2 * j + half
                            done = 2 * XT * layer + KT * k
                            row_waits = None
                            if behind_norm and not half:
                                row_waits = [done + n for n in ((1, 2, 4, 4) if k == 0 else (2, 2, 4, 4))]
                            multiply(C0[f"up{layer}"] + 2 * DC * j + DC * half + k, k,
                                     [xs[:, k * KT + kk, :] for kk in range(KT)], KT, tiles, 4 * half,
                                     first=k == 0, last=k == DC - 1, before=G - 2 if k == 0 else None,
                                     row_waits=row_waits)

                up_group(0, behind_norm=True)
                with pe.Fori(1, UJ - 1) as j:
                    up_group(j)
                up_group(UJ - 1)

                c0, g0, L = C0[f"down{layer}"], G0[f"down{layer}"], 2 * layer + 1

                def down_group(dg):
                    for k in range(FC):
                        start, rows = sum(DOWN_ROWS[:k]), DOWN_ROWS[k]
                        pe.wait_ge(inner_split, UJ * layer + (start + rows - 1) // CT + 1)
                        before = (g0 - 2 if isinstance(dg, int) and dg == 0 else g0 + dg - 1) if k == 0 else None
                        multiply(c0 + FC * dg + k, k, [gs[:, start + kk, :] for kk in range(rows)], rows,
                                 first=k == 0, last=k == FC - 1, before=before)
                        if isinstance(dg, int) and dg == 1 and k == 0:
                            find_centre(L)

                down_group(0)
                down_group(1)
                with pe.Fori(2, NG) as dg:
                    down_group(dg)
                finish_statistics(L)
                if layer == 1:
                    break

                def multiply_values(g, c, k, n):
                    for half in range(2):
                        pe.wait_ge(weights_split, 2 * c + half + 1)
                        cols = slice(half * 2 * P, half * 2 * P + 2 * P)
                        if n == 0 and half == 0 and not (isinstance(g, int) and g == 0):
                            pe.wait_ge(heads_split, 4 * g)
                        for tt in range(TT):
                            for kk in range(KT):
                                x_hi = xs[:, n * KT + kk, tt * P:tt * P + P]
                                x_lo = xs[:, n * KT + kk, T + tt * P:T + tt * P + P]
                                b, w_high, w_low = bank[4 + tt][:, cols], high[k % 2][:, kk, cols], low[k % 2][:, kk, cols]
                                nc.tensor.matmul(b, x_hi, w_high, start=n + half + kk == 0, stop=False)
                                nc.tensor.matmul(b, x_hi, w_low, start=False, stop=False)
                                op = nc.tensor.matmul(b, x_lo, w_high, start=False,
                                                      stop=(n, half, kk) == (DC - 1, 1, KT - 1))
                            op.then_inc(tiles_multiplied, 1)

                def scores(g):
                    pe.wait_ge(evacuated, 4 * (G0["qkv"] + 3 * g + 2) + 4)
                    for h in range(CT):
                        nc.tensor.matmul(bank[4 + h][:, 0:T], k_t[:, h, 0:P], q_t[:, h, :], start=True, stop=False)
                        nc.tensor.matmul(bank[4 + h][:, T:T + P], k_t[:, h, P:T], q_t[:, h, P:T], start=False,
                                         stop=True).then_inc(heads_multiplied, 1)

                def sum_softplus_parts(g):
                    pe.wait_ge(sum_weights_ready, 2)
                    pe.wait_ge(soft_split, g + 1)
                    for h in range(CT):
                        pe.wait_ge(z_copied, 4 * g + h + 1)
                        for n, part in enumerate((soft_high, soft_low)):
                            nc.tensor.matmul(bank[4 + h][:, 0:3 * P], tri_r[:, :], part[:, h, :], start=n == 0,
                                             stop=False)
                            op = nc.tensor.matmul(bank[4 + h][:, P:T], mean_r[:, :], part[:, h, T:T + P],
                                                  start=False, stop=n == 1)
                        op.then_inc(heads_multiplied, 1)

                def sum_softplus(g):
                    pe.wait_ge(masked, 4 * g + 2)
                    for h in range(CT):
                        pe.wait_ge(z_copied, 4 * g + h + 1)
                        nc.tensor.matmul(bank[4 + h][:, 0:T], tri_w[:, :], soft[:, h, 0:T], start=True, stop=False)
                        nc.tensor.matmul(bank[4 + h][:, T:T + P], tri_w[:, :], soft[:, h, T:T + P], start=False,
                                         stop=False)
                        nc.tensor.matmul(bank[4 + h][:, P:T], mean_w[:, :], soft[:, h, T:T + P], start=False,
                                         stop=True).then_inc(heads_multiplied, 1)

                def weigh_values(g):
                    pe.wait_ge(masked, 4 * g + 4)
                    for h in range(CT):
                        nc.tensor.matmul(bank[4 + h][:, 0:T], v_n[:, 0, h * P:h * P + P], z[:, h, 0:T], start=True, stop=False)
                        nc.tensor.matmul(bank[4 + h][:, P:T], v_n[:, 1, h * P:h * P + P], z[:, h, T:T + P], start=False,
                                         stop=True).then_inc(heads_multiplied, 1)

                def qkv_group(g, first=False):
                    for k in range(3 * DC):
                        part, n = k // DC, k % DC
                        start_rows = None
                        if first and part == 0:
                            start_rows = [XT + KT * k + m for m in ((1, 2, 4, 4) if k == 0 else (2, 2, 4, 4))]
                        G, c = G0["qkv"] + 3 * g + part, C0["qkv"] + 3 * DC * g + k
                        if part == 2:
                            multiply_values(g, c, k, n)
                        else:
                            before = None if n else G - 2 if part == 0 and not first else G - 1
                            multiply(c, k, [xs[:, n * KT + kk, :] for kk in range(KT)], KT,
                                     first=n == 0, last=n == DC - 1, before=before, row_waits=start_rows)
                        if not first:
                            if k == 0:
                                scores(g - 1)
                            if k == 3:
                                sum_softplus_parts(g - 1)
                            if k == 5:
                                weigh_values(g - 1)

                qkv_group(0, first=True)
                with pe.Fori(1, NG) as g:
                    qkv_group(g)

                def attn_out_group(dg):
                    for k in range(DC):
                        pe.wait_ge(heads_split, 4 * k + 4)
                        G = G0["attn_out"] + dg
                        before = None if k else G - 2 if isinstance(dg, int) and dg == 0 else G - 1
                        multiply(C0["attn_out"] + DC * dg + k, k, [gs[:, k * KT + kk, :] for kk in range(KT)], KT,
                                 first=k == 0, last=k == DC - 1, before=before,
                                 between={1: lambda: scores(NG - 1)} if isinstance(dg, int) and dg + k == 0 else None)
                        if isinstance(dg, int) and dg == 0:
                            if k == 1:
                                sum_softplus(NG - 1)
                            if k == 2:
                                weigh_values(NG - 1)
                        if isinstance(dg, int) and dg == 1 and k == 0:
                            find_centre(2)

                attn_out_group(0)
                attn_out_group(1)
                with pe.Fori(2, NG) as dg:
                    attn_out_group(dg)
                finish_statistics(2)

            for n in range(2 * NG):
                dq, tt = n // 2, n % 2
                pe.wait_ge(affine, XT * 3 + CT * dq + CT)
                if n == 0:
                    pe.wait_ge(evacuated, 4 * G0["end"])
                if n == 5:
                    pe.wait_ge(variance_ready, 4)
                for q in range(CT):
                    op = nc.tensor.transpose(bank[n][:, q * P:(q + 1) * P],
                                             r[:, CT * dq + q, tt * P:(tt + 1) * P], ident[:, :])
                op.then_inc(out_transposed, 1)


INPUTS = ["x", "pool_w", "pool_scale", "attn_w_qkv", "attn_w_o", "ffn_w_up", "ffn_conv_w", "ffn_conv_b",
          "ffn_w_down", "ln_mix_g", "ln_mix_b", "ln_ffn_g", "ln_ffn_b"]


def kernel(**inputs):
    import numpy as np
    import concourse.bacc as bacc
    from concourse.bass_utils import run_bass_kernel_spmd

    nc = bacc.Bacc("TRN2", target_bir_lowering=False, num_devices=1, dynamic_dma_scratch_size=4096)
    arrays, args = {}, []
    for name in INPUTS:
        a = np.ascontiguousarray(inputs[name])
        arrays[f"in_{name}"] = a
        args.append(nc.dram_tensor(f"in_{name}", a.shape, mybir.dt.from_np(a.dtype), kind="ExternalInput").ap())
    shape = inputs["x"].shape
    out = nc.dram_tensor("out_x", shape, mybir.dt.float32, kind="ExternalOutput").ap()
    decoder_trunk(nc, *args, out)
    result = run_bass_kernel_spmd(nc, [arrays], core_ids=[0])
    return result.results[0]["out_x"]
```
